# Optimizing a Trainium2 kernel written in Bass

```python
import math
import jax, jax.numpy as jnp
from jax import lax
import numpy as np

D_MODEL = 1024
BATCH = 1
SEQ = 1024
DEPTH = 1
DEC_BATCH = 1
DEC_SEQ = 512
PAST_LEN = 128

N_META = 16
GRID_W = 64
HEAD_DIM = 64
NA_HEADS = 8
NA_WIDTH = NA_HEADS * HEAD_DIM
NA_MAX_KH = 8
NA_KW = 16
DIFF_HEADS = 4
DIFF_WIDTH = DIFF_HEADS * 2 * HEAD_DIM
MIX_WIDTH = NA_WIDTH + DIFF_WIDTH
PROJ_WIDTH = 3 * NA_WIDTH + 3 * DIFF_WIDTH
Q_BLOCK = 128
ROPE_THETA = 10000.0
N_EXPERTS = 16
EC_CAPACITY_FACTOR = 2
D_FF_EXPERT = 2048
RMS_EPS = 1e-6
SUBLN_EPS = 1e-5

kernel_name = 'hymba_na_diffattn_ec_encoder'

def _rmsnorm(x, g, eps=RMS_EPS):
    x32 = x.astype(jnp.float32)
    y = x32 * lax.rsqrt(jnp.mean(x32 * x32, axis=-1, keepdims=True) + eps)
    return (y * g.astype(jnp.float32)).astype(x.dtype)

def _rotary(t, cos, sin):
    half = t.shape[-1] // 2
    t32 = t.astype(jnp.float32)
    t1, t2 = t32[..., :half], t32[..., half:]
    c = cos[None, :, None, None, :]
    s = sin[None, :, None, None, :]
    return jnp.concatenate([t1 * c - t2 * s, t2 * c + t1 * s], axis=-1).astype(t.dtype)

def _neighbourhood_attention(q, k, v, rpb, meta_bias):
    B, L, H, dh = q.shape
    n_real = L - N_META
    rows = n_real // GRID_W
    kh = min(NA_MAX_KH, rows)
    scale = dh ** -0.5
    qm, km, vm = q[:, :N_META], k[:, :N_META], v[:, :N_META]
    qg = q[:, N_META:].reshape(B, rows, GRID_W, H, dh)
    kg = k[:, N_META:].reshape(B, rows, GRID_W, H, dh)
    vg = v[:, N_META:].reshape(B, rows, GRID_W, H, dh)
    r_idx = jnp.arange(rows)
    row_start = jnp.clip(r_idx - kh // 2, 0, rows - kh)
    c_idx = jnp.arange(GRID_W)
    col_idx = jnp.clip(c_idx - NA_KW // 2, 0, GRID_W - NA_KW)[:, None] + jnp.arange(NA_KW)
    col_off = col_idx - c_idx[:, None] + NA_KW - 1
    mb = meta_bias.astype(jnp.float32)

    s_mm = jnp.einsum('bqhd,bkhd->bhqk', qm, km).astype(jnp.float32) * scale + mb[None, :, None, :]
    out_meta = jnp.einsum('bhqk,bkhd->bqhd', jax.nn.softmax(s_mm, axis=-1).astype(v.dtype), vm)

    def row_fn(args):
        qr, r, rs = args
        kr = lax.dynamic_slice_in_dim(kg, rs, kh, axis=1)[:, :, col_idx]
        vr = lax.dynamic_slice_in_dim(vg, rs, kh, axis=1)[:, :, col_idx]
        row_off = rs + jnp.arange(kh) - r + NA_MAX_KH - 1
        bias = rpb[:, row_off[:, None, None], col_off[None]]
        bias = bias.transpose(0, 2, 1, 3).reshape(H, GRID_W, kh * NA_KW).astype(jnp.float32)
        s_loc = jnp.einsum('bqhd,bkqjhd->bhqkj', qr, kr).reshape(B, H, GRID_W, kh * NA_KW)
        s_loc = s_loc.astype(jnp.float32) * scale + bias[None]
        s_met = jnp.einsum('bqhd,bmhd->bhqm', qr, km).astype(jnp.float32) * scale + mb[None, :, None, :]
        p = jax.nn.softmax(jnp.concatenate([s_loc, s_met], axis=-1), axis=-1).astype(v.dtype)
        p_loc = p[..., :kh * NA_KW].reshape(B, H, GRID_W, kh, NA_KW)
        p_met = p[..., kh * NA_KW:]
        return (jnp.einsum('bhqkj,bkqjhd->bqhd', p_loc, vr)
                + jnp.einsum('bhqm,bmhd->bqhd', p_met, vm))

    out = lax.map(row_fn, (qg.transpose(1, 0, 2, 3, 4), r_idx, row_start))
    out = out.transpose(1, 0, 2, 3, 4).reshape(B, n_real, H, dh)
    return jnp.concatenate([out_meta, out], axis=1).reshape(B, L, H * dh)

def _diff_attention(q, k, v, lam, lambda_init, subln):
    B, L, H, _, dh = q.shape
    scale = dh ** -0.5

    def attend(qb):
        s = jnp.einsum('bqhcd,bkhcd->bhcqk', qb, k).astype(jnp.float32) * scale
        p = jax.nn.softmax(s, axis=-1)
        a = (p[:, :, 0] - lam * p[:, :, 1]).astype(v.dtype)
        return jnp.einsum('bhqk,bkhe->bqhe', a, v)

    n_real = L - N_META
    nblk = n_real // Q_BLOCK
    out_meta = attend(q[:, :N_META])
    qb = q[:, N_META:].reshape(B, nblk, Q_BLOCK, H, 2, dh).transpose(1, 0, 2, 3, 4, 5)
    out_real = lax.map(attend, qb).transpose(1, 0, 2, 3, 4).reshape(B, n_real, H, 2 * dh)
    o = jnp.concatenate([out_meta, out_real], axis=1)
    o = _rmsnorm(o, subln, SUBLN_EPS) * (1.0 - lambda_init)
    return o.reshape(B, L, H * 2 * dh)

def _expert_choice_ffn(h, w_router, w_gate, w_up, w_down):
    B, L, D = h.shape
    n_tok = B * L
    hf = h.reshape(n_tok, D)
    affinity = jax.nn.softmax((hf @ w_router).astype(jnp.float32), axis=-1)
    cap = EC_CAPACITY_FACTOR * n_tok // N_EXPERTS
    gate, idx = lax.top_k(affinity.T, cap)
    xe = hf[idx]
    a = jnp.einsum('ecd,edf->ecf', xe, w_gate)
    b = jnp.einsum('ecd,edf->ecf', xe, w_up)
    ye = jnp.einsum('ecf,efd->ecd', jax.nn.silu(a) * b, w_down) * gate[..., None].astype(h.dtype)
    out = jnp.zeros_like(hf).at[idx.reshape(-1)].add(ye.reshape(-1, D))
    return out.reshape(B, L, D)

def _layer(x, layer_idx, cos, sin, norm_mix, w_in, na_rpb, na_meta_bias, lambda_q1, lambda_k1,
           lambda_q2, lambda_k2, diff_subln, w_out, norm_ffn, w_router, w_gate, w_up, w_down):
    B, L, D = x.shape
    h = _rmsnorm(x, norm_mix)
    proj = h @ w_in
    splits = [NA_WIDTH, 2 * NA_WIDTH, 3 * NA_WIDTH, 3 * NA_WIDTH + DIFF_WIDTH, 3 * NA_WIDTH + 2 * DIFF_WIDTH]
    na_q, na_k, na_v, d_q, d_k, d_v = jnp.split(proj, splits, axis=-1)

    na_out = _neighbourhood_attention(na_q.reshape(B, L, NA_HEADS, HEAD_DIM),
                                      na_k.reshape(B, L, NA_HEADS, HEAD_DIM),
                                      na_v.reshape(B, L, NA_HEADS, HEAD_DIM),
                                      na_rpb, na_meta_bias)

    lambda_init = 0.8 - 0.6 * math.exp(-0.3 * layer_idx)
    lam = (jnp.exp(jnp.sum(lambda_q1.astype(jnp.float32) * lambda_k1.astype(jnp.float32)))
           - jnp.exp(jnp.sum(lambda_q2.astype(jnp.float32) * lambda_k2.astype(jnp.float32)))
           + lambda_init)
    dq = _rotary(d_q.reshape(B, L, DIFF_HEADS, 2, HEAD_DIM), cos, sin)
    dk = _rotary(d_k.reshape(B, L, DIFF_HEADS, 2, HEAD_DIM), cos, sin)
    dv = d_v.reshape(B, L, DIFF_HEADS, 2 * HEAD_DIM)
    diff_out = _diff_attention(dq, dk, dv, lam, lambda_init, diff_subln)

    x = x + jnp.concatenate([na_out, diff_out], axis=-1) @ w_out
    x = x + _expert_choice_ffn(_rmsnorm(x, norm_ffn), w_router, w_gate, w_up, w_down)
    return x

def _encode(x, meta_tokens, norm_mix, w_in, na_rpb, na_meta_bias, lambda_q1, lambda_k1, lambda_q2,
            lambda_k2, diff_subln, w_out, norm_ffn, w_router, w_gate, w_up, w_down, final_norm):
    B, T, D = x.shape
    L = N_META + T
    meta = jnp.broadcast_to(meta_tokens.astype(x.dtype)[None], (B, N_META, D))
    h = jnp.concatenate([meta, x], axis=1)
    pos = jnp.arange(L, dtype=jnp.float32)
    inv_freq = 1.0 / (ROPE_THETA ** (jnp.arange(0, HEAD_DIM, 2, dtype=jnp.float32) / HEAD_DIM))
    ang = pos[:, None] * inv_freq[None, :]
    cos, sin = jnp.cos(ang), jnp.sin(ang)
    for l in range(DEPTH):
        h = _layer(h, l, cos, sin, norm_mix[l], w_in[l], na_rpb[l], na_meta_bias[l], lambda_q1[l],
                   lambda_k1[l], lambda_q2[l], lambda_k2[l], diff_subln[l], w_out[l], norm_ffn[l],
                   w_router[l], w_gate[l], w_up[l], w_down[l])
    return _rmsnorm(h, final_norm)[:, N_META:]

def setup_inputs(seed: int = 0) -> dict:
    key = jax.random.key(seed)
    ks = jax.random.split(key, 20)
    f32 = jnp.float32
    nrm = lambda k, shape, s: jax.random.normal(k, shape, f32) * s
    return {
        'x_prompt': nrm(ks[0], (BATCH, SEQ, D_MODEL), 1.0),
        'x_sample': nrm(ks[1], (DEC_BATCH, DEC_SEQ, D_MODEL), 1.0),
        'meta_tokens': nrm(ks[2], (N_META, D_MODEL), 1.0),
        'norm_mix': 1.0 + nrm(ks[3], (DEPTH, D_MODEL), 0.01),
        'w_in': nrm(ks[4], (DEPTH, D_MODEL, PROJ_WIDTH), D_MODEL ** -0.5),
        'na_rpb': nrm(ks[5], (DEPTH, NA_HEADS, 2 * NA_MAX_KH - 1, 2 * NA_KW - 1), 0.02),
        'na_meta_bias': nrm(ks[6], (DEPTH, NA_HEADS, N_META), 0.02),
        'lambda_q1': nrm(ks[7], (DEPTH, HEAD_DIM), 0.1),
        'lambda_k1': nrm(ks[8], (DEPTH, HEAD_DIM), 0.1),
        'lambda_q2': nrm(ks[9], (DEPTH, HEAD_DIM), 0.1),
        'lambda_k2': nrm(ks[10], (DEPTH, HEAD_DIM), 0.1),
        'diff_subln': 1.0 + nrm(ks[11], (DEPTH, 2 * HEAD_DIM), 0.01),
        'w_out': nrm(ks[12], (DEPTH, MIX_WIDTH, D_MODEL), MIX_WIDTH ** -0.5),
        'norm_ffn': 1.0 + nrm(ks[13], (DEPTH, D_MODEL), 0.01),
        'w_router': nrm(ks[14], (DEPTH, D_MODEL, N_EXPERTS), D_MODEL ** -0.5),
        'w_gate': nrm(ks[15], (DEPTH, N_EXPERTS, D_MODEL, D_FF_EXPERT), D_MODEL ** -0.5),
        'w_up': nrm(ks[16], (DEPTH, N_EXPERTS, D_MODEL, D_FF_EXPERT), D_MODEL ** -0.5),
        'w_down': nrm(ks[17], (DEPTH, N_EXPERTS, D_FF_EXPERT, D_MODEL), D_FF_EXPERT ** -0.5),
        'final_norm': 1.0 + nrm(ks[18], (D_MODEL,), 0.01),
    }

def reference(x_prompt, x_sample, meta_tokens, norm_mix, w_in, na_rpb, na_meta_bias, lambda_q1,
              lambda_k1, lambda_q2, lambda_k2, diff_subln, w_out, norm_ffn, w_router, w_gate, w_up,
              w_down, final_norm):
    y_prompt = _encode(x_prompt, meta_tokens, norm_mix, w_in, na_rpb, na_meta_bias, lambda_q1,
                       lambda_k1, lambda_q2, lambda_k2, diff_subln, w_out, norm_ffn, w_router,
                       w_gate, w_up, w_down, final_norm)
    y_sample = _encode(x_sample, meta_tokens, norm_mix, w_in, na_rpb, na_meta_bias, lambda_q1,
                       lambda_k1, lambda_q2, lambda_k2, diff_subln, w_out, norm_ffn, w_router,
                       w_gate, w_up, w_down, final_norm)
    return (y_prompt, y_sample)


_drawn_inputs = setup_inputs


def setup_inputs(seed=0):
    import zlib

    import numpy as np

    out = dict(_drawn_inputs(seed))
    spreads = {}
    factors = {'norm_mix': 4.65,
     'na_rpb': 8.0,
     'na_meta_bias': 8.0,
     'lambda_k1': 14.103,
     'lambda_q2': 5.126,
     'lambda_k2': 8.0,
     'diff_subln': 6.807,
     'norm_ffn': 4.663,
     'final_norm': 33.461,
     'lambda_q1': 4.076}
    for name, (base, spread) in spreads.items():
        noise = np.random.default_rng([zlib.crc32(name.encode()), seed]).standard_normal(out[name].shape)
        drawn = base * np.exp(spread * noise) if base else spread * noise
        out[name] = __import__('jax').numpy.asarray(drawn.astype(out[name].dtype))
    for name, factor in factors.items():
        out[name] = (out[name] * factor).astype(out[name].dtype)
    return out
```

```python
from contextlib import ExitStack

import numpy as np

import concourse.bass as bass
from concourse import mybir

f32 = mybir.dt.float32
f32r = mybir.dt.float32r
u32 = mybir.dt.uint32
ALU = mybir.AluOpType
ACT = mybir.ActivationFunctionType
AX = mybir.AxisListType

P = 128
D = 1024
KD = D // P
N_META = 16
GRID_W = 64
DH = 64
NA_HEADS = 8
N_PROMPT, N_SAMPLE = 1024, 512
N_REAL = N_PROMPT + N_SAMPLE
FULL = N_REAL // P
TAIL = 2 * N_META
NTOK = N_REAL + TAIL
NT = FULL + 1
PT = N_PROMPT // P
NA_W = 512
PROJ = 3072
UNITS = 4
N_EXP = 16
D_FF = 2048
CAP_P = 2 * (N_PROMPT + N_META) // N_EXP
CAP_S = 2 * (N_SAMPLE + N_META) // N_EXP
SLOTS = CAP_P + CAP_S
HS = SLOTS // 2
KH, KW = 8, 16
MASKED = -1e30
RMS_EPS, SUB_EPS = 1e-6, 1e-5
LAMBDA_INIT = 0.2
QCH = NTOK // 4
FCH = 256
NCH = D_FF // FCH
FT = FCH // P


def na_steps():
    out = []
    for a in range(2):
        for t in range(FULL):
            first, tiles = (0, PT) if t < PT else (PT, FULL - PT)
            i = t - first
            k0 = min(max(i - 2, 0), tiles - 4)
            ninth = first + k0 + 4 if 2 <= i <= tiles - 3 else None
            out.append((a, t, P, first + k0, ninth, 2 * k0 - 2 * i + KH - 1))
        out.append((a, FULL, TAIL, None, None, 0))
    return out


def diff_steps():
    out = [(t, P, P, 0, PT) for t in range(PT)]
    out += [(t, P, P, PT, FULL - PT) for t in range(PT, FULL)]
    out += [(FULL, TAIL, TAIL, PT, FULL - PT), (FULL, TAIL, N_META, 0, PT)]
    return out


class Chain:

    def __init__(self, sem):
        self.sem, self.base, self.n, self.total = sem, 0, 0, 0

    def enter(self, i, per):
        self.per, self.base, self.n = per, self.total + i * per, 0

    def leave(self, turns):
        assert self.n == self.per, (self.n, self.per)
        self.total += turns * self.per
        self.base, self.n = self.total, 0

    def mark(self, ins):
        ins.then_inc(self.sem, 1)
        self.n += 1

    def settle(self, eng):
        eng.wait_ge(self.sem, self.base + self.n)

    def flat(self):
        self.total = self.base + self.n
        self.base, self.n = self.total, 0


def build(nc, x_all, w_in, w_out, w_router, w_gate, w_up, w_down, rpb, meta_bias, lambdas, vecs,
          final_norm, rope, ident_in, y):
    acc_d = nc.dram_tensor("residual_rows", (NTOK, D), f32, kind="Internal").ap()
    h_d = nc.dram_tensor("normed_rows", (NTOK, D), f32, kind="Internal").ap()
    ROFF = 2 * KH - 1
    COFF = 2 * KW - 1
    bias_h = nc.dram_tensor("column_bias", (GRID_W, NA_HEADS, ROFF, GRID_W), f32, kind="Internal")
    bias_d = bias_h.ap()

    ctx = ExitStack()
    with ctx:
        start = 16640
        limit = 229344
        spans = []

        def at(name, shape, off, dt=f32):
            size = int(np.prod(shape[1:])) * 4
            assert start <= off and off + size <= limit, (name, off, size)
            spans.append((off, off + size, name))
            return nc.alloc_sbuf_tensor_at(name, list(shape), dt, offset=off)

        class Region:
            def __init__(self, off):
                self.off = off

            def __call__(self, name, shape, dt=f32):
                t = at(name, shape, self.off, dt)
                self.off += (int(np.prod(shape[1:])) * 4 + 31) // 32 * 32
                return t

        R = Region(start)
        ident = R("ident", [P, P])
        vec = R("vec", [P, 3 * KD])
        lam4 = R("lam4", [P, 4, DH])
        neglam = R("neglam", [P, 1])
        lam_s = R("lam_s", [P, 2])
        lam_e = R("lam_e", [P, 2])
        lam_t = R("lam_t", [P, 2, DH])
        half_neg = R("half_neg", [P, 4])
        ms = R("ms", [P, 2, 1])
        ms2 = R("ms2", [P, 2, 1])
        rstd = R("rstd", [P, 2, 1])
        nmax = R("nmax", [P, 2, 2])
        mx0 = R("mx0", [P, 2, 1])
        ssum = R("ssum", [P, 4, 2])
        rec = R("rec", [P, 4, 2])
        gate_cur = R("gate_cur", [HS, 2])
        e_sq = R("e_sq", [P, 2, P])
        sr = R("sr", [P, 2, 1])
        idxT = R("idxT", [HS, 2, N_EXP + 1], u32)
        gateT = R("gateT", [HS, 2, N_EXP + 1])
        idx_gather = R("idx_gather", [HS, 2], u32)
        idx_scatter = R("idx_scatter", [HS, 2], u32)
        const_end = R.off

        R = Region(const_end)
        hT = R("hT", [P, KD, NTOK])
        mix = R("mix", [P, NT, D])
        after_mix = R.off
        wqkv = R("wqkv", [P, KD, 3 * P])
        qT = R("qT", [P, NTOK])
        kT = R("kT", [P, NTOK])
        v = R("v", [P, NT, P])
        cos = R("cos", [P, NTOK])
        sin = R("sin", [P, NTOK])
        ms_d = R("ms_d", [P, NT, UNITS])
        rstd_d = R("rstd_d", [P, NT, UNITS])
        kind_off = R.off
        R = Region(kind_off)
        bias_i = R("bias_i", [P, 2, 592])
        bias_e = R("bias_e", [P, 2, 14, GRID_W])
        s2 = R("s2", [P, 2, 592])
        e_na = R("e_na", [P, 2, 592])
        et_na = R("et_na", [P, 2, 768])
        mask_fill = R("mask_fill", [P, 960])
        R = Region(kind_off)
        q_raw = R("q_raw", [P, NTOK])
        k_raw = R("k_raw", [P, NTOK])
        q_swp = R("q_swp", [P, NTOK])
        k_swp = R("k_swp", [P, NTOK])
        e_df = R("e_df", [P, 2, 2, N_PROMPT + N_META])
        et_df = R("et_df", [P, 2, 9 * P])
        nsm = R("nsm", [P, 2, NT * N_META])
        nmm = R("nmm", [P, 2, NT])
        R = Region(after_mix)
        xt = R("xt", [P, 2, D])
        xn = R("xn", [P, 2, D])
        junk = R("junk", [P, 2, D])

        R = Region(const_end)
        w_out_sb = R("w_out_sb", [P, KD, D])
        w_rt = R("w_rt", [P, KD, N_EXP])
        assert R.off <= const_end + KD * NTOK * 4
        R = Region(kind_off)
        mixs = R("mixs", [P, 2, D])
        mixT = R("mixT", [P, 2, KD, P])
        xr = R("xr", [P, 2, D])
        x2 = R("x2", [P, 2, D])
        xn2 = R("xn2", [P, 2, D])
        h2T = R("h2T", [P, 2, KD, P])
        aff_end = R.off
        R = Region(after_mix)
        aff_all = R("aff_all", [N_EXP, NTOK])
        aff = R("aff", [48, N_PROMPT + N_META])
        junk2 = R("junk2", [P, 2, D])
        lg_e = R("lg_e", [P, 2, N_EXP])
        lg_a = R("lg_a", [P, 2, N_EXP])
        top_v = R("top_v", [48, 136])
        top_i = R("top_i", [48, 136], u32)
        top_f = R("top_f", [48, 136])
        top_m = R("top_m", [48, 136])
        slot_r = R("slot_r", [N_EXP, SLOTS])
        slot_g = R("slot_g", [N_EXP, SLOTS])
        assert R.off <= kind_off - 2 * NT * UNITS * 4 - 64

        R = Region(const_end)
        raw = R("raw", [P, 2, 3, 2048])
        w_hi = R("w_hi", [P, 2, 3, 2048], f32r)
        w_lo = R("w_lo", [P, 2, 3, 2048], f32r)
        xg = R("xg", [HS, 2, D])
        xe_hi = R("xe_hi", [P, KD, SLOTS], f32r)
        xe_lo = R("xe_lo", [P, KD, SLOTS], f32r)
        yT = R("yT", [P, KD, SLOTS])
        ye = R("ye", [HS, 2, D])
        sil = R("sil", [P, 2, SLOTS])
        hf = R("hf", [P, 2, SLOTS])
        a_hi = R("a_hi", [P, 2, FT, SLOTS], f32r)
        a_lo = R("a_lo", [P, 2, FT, SLOTS], f32r)
        R = Region(const_end)
        g_fin = R("g_fin", [P, D])
        xf = R("xf", [P, FULL, D])
        yo = R("yo", [P, 2, D])
        junk3 = R("junk3", [P, 2, D])

        ps = ctx.enter_context(nc.psum_tensor("ps", [P, 8 * 512], f32))
        BANK = 512

        def sem(name):
            return ctx.enter_context(nc.semaphore(name))

        dve_own, act_own = sem("dve_own"), sem("act_own")
        const_in = sem("const_in")
        consts_dve = sem("consts_dve")
        lam_dot, lam_exp = sem("lam_dot"), sem("lam_exp")
        x_in = [sem(f"x_in{b}") for b in range(2)]
        ss_ready, ms_ready, rstd_ready = sem("ss_ready"), sem("ms_ready"), sem("rstd_ready")
        xn_ready, xT_ready, h_ready = sem("xn_ready"), sem("xT_ready"), sem("h_ready")
        w_qkv_in, pj_ready = sem("w_qkv_in"), sem("pj_ready")
        qk_evac, v_evac = sem("qk_evac"), sem("v_evac")
        fill_ready, fill_in, diag_in = sem("fill_ready"), sem("fill_in"), sem("diag_in")
        mask_ready, bias_in = sem("mask_ready"), sem("bias_in")
        na_s, na_sb, na_e, na_t = sem("na_s"), sem("na_sb"), sem("na_e"), sem("na_t")
        na_et_a, na_et_d, na_o, na_mix = sem("na_et_a"), sem("na_et_d"), sem("na_o"), sem("na_mix")
        swp_in, qk_rot = sem("swp_in"), sem("qk_rot")
        df_ms, df_msn = sem("df_ms"), sem("df_msn")
        df_s, df_m, df_e, df_c = sem("df_s"), sem("df_m"), sem("df_e"), sem("df_c")
        df_t, df_et_a, df_et_d = sem("df_t"), sem("df_et_a"), sem("df_et_d")
        df_o, df_mix, df_sq = sem("df_o"), sem("df_mix"), sem("df_sq")
        w_out_in, sub_ms, sub_rstd = sem("w_out_in"), sem("sub_ms"), sem("sub_rstd")
        mixs_a, mixs_d, mT_ready, mT_evac = sem("mixs_a"), sem("mixs_d"), sem("mT_ready"), sem("mT_evac")
        xr_in = [sem(f"xr_in{b}") for b in range(2)]
        o_ready, x2_ready = sem("o_ready"), sem("x2_ready")
        x2_out = [sem(f"x2_out{b}") for b in range(2)]
        xn2_out = [sem(f"xn2_out{b}") for b in range(2)]
        ss2_ready, ms2_ready, rstd2_ready = sem("ss2_ready"), sem("ms2_ready"), sem("rstd2_ready")
        xn2_ready, h2_ready, h2_evac = sem("xn2_ready"), sem("h2_ready"), sem("h2_evac")
        lg_ready, lg_max, lg_exp, lg_aff = sem("lg_ready"), sem("lg_max"), sem("lg_exp"), sem("lg_aff")
        affT_ready, affT_evac = sem("affT_ready"), sem("affT_evac")
        slots_ready, slotT_ready, idx_ready = sem("slots_ready"), sem("slotT_ready"), sem("idx_ready")
        raw_in = [[sem(f"raw_in{b}{j}") for j in range(3)] for b in range(2)]
        hi_done, lo_done, dn_used = sem("hi_done"), sem("lo_done"), sem("dn_used")
        idx_cp, gather_in = sem("idx_cp"), sem("gather_in")
        xgT_ready, xe_hi_done, xe_lo_done = sem("xgT_ready"), sem("xe_hi_done"), sem("xe_lo_done")
        gu_ready, silu_done, act_f, act_hi, act_lo = (sem("gu_ready"), sem("silu_done"), sem("act_f"),
                                                       sem("act_hi"), sem("act_lo"))
        y_ready, yT_a, yT_d, yt_ready = sem("y_ready"), sem("yT_a"), sem("yT_d"), sem("yt_ready")
        ye_a, ye_d, gate_cp = sem("ye_a"), sem("ye_d"), sem("gate_cp")
        idx_sc, scatter_out = sem("idx_sc"), sem("scatter_out")
        g_in = sem("g_in")
        xf_in = [sem(f"xf_in{n}") for n in range(FULL // 2)]
        ss3, ms3, rstd3, y3 = sem("ss3"), sem("ms3"), sem("rstd3"), sem("y3")
        y_out = [sem(f"y_out{b}") for b in range(2)]

        block = ctx.enter_context(nc.Block())

        passed = {e.engine: sem(f"passed_{n}") for n, e in
                  (("act", nc.scalar), ("dve", nc.vector), ("pe", nc.tensor), ("pool", nc.gpsimd))}

        def apart(eng):
            eng.sem_inc(passed[eng.engine], 1)

        NA = na_steps()
        DF = diff_steps()
        NS, DS = len(NA), len(DF)
        PAIRS = FULL // 2
        w_in_v = w_in.rearrange("(k p) n -> p k n", p=P)
        w_out_v = w_out.rearrange("(k p) n -> p k n", p=P)

        def bcast(handle, off, dims):
            row = int(np.prod(handle.shape[1:]))
            return bass.AP(tensor=handle, offset=off, ap=[[row, handle.shape[0]]] + dims)

        @block.sync
        def _(sp):
            sp.dma_start(ident[:, :], ident_in).then_inc(const_in, 16)
            sp.dma_start(vec[:, :], vecs).then_inc(const_in, 16)
            sp.dma_start(lam4[:, :, :], lambdas.partition_broadcast(P)).then_inc(const_in, 16)
            sp.dma_start(cos[:, :], rope[0]).then_inc(const_in, 16)
            sp.dma_start(sin[:, :], rope[1]).then_inc(const_in, 16)

            with sp.Fori(0, PAIRS) as i:
                for b in range(2):
                    sp.wait_ge(xn_ready, 2 * i)
                    sp.dma_start(xt[:, b, :], x_all[bass.ds((2 * i + b) * P, P), :]).then_inc(x_in[b], 16)
            sp.wait_ge(xn_ready, 2 * PAIRS)
            sp.dma_start(xt[0:TAIL, 0, :], x_all[N_REAL:NTOK, :]).then_inc(x_in[0], 16)

            flat = GRID_W * NA_HEADS * ROFF * GRID_W
            sp.wait_ge(fill_ready, 1)
            for n in range(flat // (P * 960)):
                dst = bass.AP(tensor=bias_h, offset=n * P * 960, ap=[[960, P], [1, 960]])
                sp.dma_start(dst, mask_fill[:, :]).then_inc(fill_in, 16)
            sp.wait_ge(fill_in, 16 * (flat // (P * 960)))
            row = NA_HEADS * ROFF * GRID_W
            hr = NA_HEADS * ROFF
            last_ws = GRID_W - KW
            mid0, mid1 = KW // 2, last_ws + KW // 2
            runs = [(c, 1, 0) for c in range(mid0)] + [(mid0, mid1 - mid0 + 1, 0)]
            runs += [(c, 1, last_ws) for c in range(mid1 + 1, GRID_W)]
            for c, n, ws in runs:
                first_off = ws - c + KW - 1
                src = bass.AP(tensor=rpb.tensor, offset=first_off, ap=[[COFF, hr], [1, KW]])
                dst = bass.AP(tensor=bias_h, offset=c * row + ws, ap=[[GRID_W, hr], [1, KW]])
                if n > 1:
                    src = bass.AP(tensor=rpb.tensor, offset=first_off, ap=[[0, n], [COFF, hr], [1, KW]])
                    dst = bass.AP(tensor=bias_h, offset=c * row + ws, ap=[[row + 1, n], [GRID_W, hr], [1, KW]])
                sp.dma_start(dst, src).then_inc(diag_in, 16)
            sp.wait_ge(diag_in, 16 * len(runs))

            sp.wait_ge(mask_ready, 1)
            with sp.Fori(0, UNITS) as u:
                sp.wait_ge(pj_ready, 12 * u)
                for j in range(3):
                    sp.dma_start(wqkv[:, :, j * P:(j + 1) * P],
                                 w_in_v[:, :, bass.ds(j * NA_W + u * P, P)]).then_inc(w_qkv_in, 16)
                sp.wait_ge(na_sb, NS * u)
                for a in range(2):
                    h = bass.ds(2 * u + a, 1)
                    lo, up = bias_d[:, h, :, :], bias_d[:, h, :, :]
                    for dst, src in (
                        (bias_e[0:64, a, :, :], lo[:, :, 1:15, :]),
                        (bias_e[64:128, a, :, :], up[:, :, 0:14, :]),
                        (bias_i[0:64, a, 0:512].rearrange("p (t k) -> p t k", k=GRID_W), lo[:, :, 3:11, :]),
                        (bias_i[64:128, a, 64:512].rearrange("p (t k) -> p t k", k=GRID_W), up[:, :, 3:10, :]),
                        (bias_i[64:128, a, 528:592].rearrange("p (t k) -> p t k", k=GRID_W), up[:, :, 10:11, :]),
                    ):
                        sp.dma_start(dst, src.rearrange("c h t k -> c (h t) k")).then_inc(bias_in, 16)
                    sp.dma_start(bias_i[:, a, 512:528],
                                 meta_bias[h, :].rearrange("a m -> (a m)").partition_broadcast(P)).then_inc(bias_in, 16)
            with sp.Fori(0, UNITS) as u:
                sp.wait_ge(pj_ready, 12 * u + 12 * UNITS)
                for j in range(3):
                    sp.dma_start(wqkv[:, :, j * P:(j + 1) * P],
                                 w_in_v[:, :, bass.ds(3 * NA_W + j * NA_W + u * P, P)]).then_inc(w_qkv_in, 16)
                sp.wait_ge(qk_evac, 8 * u + 8 * UNITS + 8)
                for src, dst in ((q_raw, q_swp), (k_raw, k_swp)):
                    for g in range(4):
                        o = g ^ 1
                        sp.dma_start(dst[32 * g:32 * g + 32, :], src[32 * o:32 * o + 32, :]).then_inc(swp_in, 16)

            sp.wait_ge(pj_ready, 12 * 2 * UNITS)
            sp.dma_start(w_out_sb[:, :, :], w_out_v).then_inc(w_out_in, 16)
            sp.dma_start(w_rt[:, :, :], w_router).then_inc(w_out_in, 16)
            sp.wait_ge(df_sq, DS * UNITS)
            with sp.Fori(0, PAIRS) as i:
                for b in range(2):
                    sp.wait_ge(x2_ready, 2 * i)
                    sp.dma_start(xr[:, b, :], x_all[bass.ds((2 * i + b) * P, P), :]).then_inc(xr_in[b], 16)
                for b in range(2):
                    sp.wait_ge(x2_ready, 2 * i + b + 1)
                    sp.dma_start(acc_d[bass.ds((2 * i + b) * P, P), :], x2[:, b, :]).then_inc(x2_out[b], 16)
                for b in range(2):
                    sp.wait_ge(xn2_ready, 2 * i + b + 1)
                    sp.dma_start(h_d[bass.ds((2 * i + b) * P, P), :], xn2[:, b, :]).then_inc(xn2_out[b], 16)
            sp.dma_start(xr[0:TAIL, 0, :], x_all[N_REAL:NTOK, :]).then_inc(xr_in[0], 16)
            sp.wait_ge(x2_ready, FULL + 1)
            sp.dma_start(acc_d[N_REAL:NTOK, :], x2[0:TAIL, 0, :]).then_inc(x2_out[0], 16)
            sp.wait_ge(xn2_ready, FULL + 1)
            sp.dma_start(h_d[N_REAL:NTOK, :], xn2[0:TAIL, 0, :]).then_inc(xn2_out[0], 16)

            sp.wait_ge(lg_ready, NT)
            with sp.Fori(0, N_EXP) as e:
                for c in range(NCH):
                    b = c % 2
                    sp.wait_ge(lo_done, 3 * NCH * e + 3 * (c + 1))
                    for j, w in ((0, w_gate), (1, w_up)):
                        sp.dma_start(raw[:, b, j, :].rearrange("p (k f) -> p k f", f=FCH),
                                     w[bass.ds(e, 1), :, c * FCH:(c + 1) * FCH]
                                     .rearrange("o (k p) f -> p (o k) f", p=P)).then_inc(raw_in[b][j], 16)
                    sp.dma_start(raw[:, b, 2, :].rearrange("p (m n) -> p m n", n=D),
                                 w_down[bass.ds(e, 1), c * FCH:(c + 1) * FCH, :]
                                 .rearrange("o (m p) n -> p (o m) n", p=P)).then_inc(raw_in[b][2], 16)

            sp.wait_ge(scatter_out, 32 * N_EXP)
            sp.dma_start(g_fin[:, :], final_norm.partition_broadcast(P)).then_inc(g_in, 16)
            for n in range(PAIRS):
                sp.dma_start(xf[:, 2 * n:2 * n + 2, :],
                             acc_d[2 * n * P:(2 * n + 2) * P, :].rearrange("(t p) d -> p t d", p=P)).then_inc(xf_in[n], 16)
            with sp.Fori(0, PAIRS) as i:
                for b in range(2):
                    sp.wait_ge(y3, 2 * i + b + 1)
                    sp.dma_start(y[bass.ds((2 * i + b) * P, P), :], yo[:, b, :]).then_inc(y_out[b], 16)
            for b in range(2):
                sp.wait_ge(y_out[b], 16 * PAIRS)

        @block.scalar
        def _(act):
            own = Chain(act_own)

            def copy(out, in_, scale=1.0):
                return act.activation(out, in_, ACT.Copy, scale=scale)

            act.wait_ge(lam_dot, 2)
            act.activation(lam_e[:, :], lam_s[:, :], ACT.Exp).then_inc(lam_exp, 1)

            def a_tile(b, count, rows):
                act.wait_ge(x_in[b], count)
                act.activation(junk[0:rows, b, :], xt[0:rows, b, :], ACT.Square,
                               accum_out=ms[0:rows, b, :]).then_inc(ss_ready, 1)

            with act.Fori(0, PAIRS) as i:
                for b in range(2):
                    act.wait_ge(rstd_ready, 2 * i)
                    a_tile(b, 16 * i + 16, P)
            act.wait_ge(rstd_ready, 2 * PAIRS)
            a_tile(0, 16 * PAIRS + 16, TAIL)

            def evac_qk(base, q_dst, k_dst):
                for n in range(8):
                    c, which = n // 2, n % 2
                    act.wait_ge(pj_ready, base + n + 1)
                    src = ps[:, (6 + n % 2) * BANK:(6 + n % 2) * BANK + QCH]
                    dst = (q_dst, k_dst)[which]
                    copy(dst[:, c * QCH:(c + 1) * QCH], src, DH ** -0.5 if which == 0 else 1.0).then_inc(qk_evac, 1)

            with act.Fori(0, UNITS) as u:
                evac_qk(u * 12, qT, kT)
                for s in range(NS + 2):
                    if s >= 2:
                        n = s - 2
                        a, t, rows, k0, ninth, _ = NA[n]
                        act.wait_ge(na_t, u * NS + n + 1)
                        if n >= 2:
                            act.wait_ge(na_o, u * NS + n - 1)
                        if k0 is not None:
                            copy(et_na[:, n % 2, 0:512], ps[:, 4 * BANK:5 * BANK]).then_inc(na_et_a, 1)
                    if s < NS:
                        a, t, rows, k0, ninth, _ = NA[s]
                        act.wait_ge(na_sb, u * NS + s + 1)
                        if s >= 2:
                            act.wait_ge(na_t, u * NS + s - 1)
                        if s >= 4:
                            act.wait_ge(na_mix, u * NS + s - 3)
                        cols = slice(512, 528) if k0 is None else slice(0, 592 if ninth is not None else 528)
                        act.activation(e_na[0:rows, s % 2, cols], s2[0:rows, s % 2, cols], ACT.Exp,
                                       bias=nmax[0:rows, s % 2, 0:1], scale=-1.0,
                                       accum_out=ssum[0:rows, s % 4, 0:1]).then_inc(na_e, 1)

            with act.Fori(0, UNITS) as u:
                act.wait_ge(na_mix, NS * UNITS)
                act.wait_ge(qk_rot, 2 * u)
                evac_qk(u * 12 + 12 * UNITS, q_raw, k_raw)
                for s in range(DS + 3):
                    if 0 <= s - 2 < DS:
                        n = s - 2
                        t, rows, keep, k0, kt = DF[n]
                        act.wait_ge(df_t, u * DS + n + 1)
                        if n >= 2:
                            act.wait_ge(df_o, u * DS + n - 1)
                        copy(et_df[:, n % 2, 0:4 * P].rearrange("p (j r) -> p j r", r=P)[:, :, 0:rows],
                             ps[:, 4 * BANK:5 * BANK].rearrange("p (j r) -> p j r", r=P)[:, :, 0:rows]).then_inc(df_et_a, 1)
                    if s < DS:
                        t, rows, keep, k0, kt = DF[s]
                        w = kt * P + N_META
                        if s >= 2:
                            act.wait_ge(df_t, u * DS + s - 1)
                        for c in range(2):
                            act.wait_ge(df_m, 2 * (u * DS + s) + c + 1)
                            act.activation(e_df[0:rows, s % 2, c, 0:w], e_df[0:rows, s % 2, c, 0:w],
                                           ACT.Exp, bias=nmax[0:rows, s % 2, c:c + 1], scale=-1.0,
                                           accum_out=ssum[0:rows, s % 4, c:c + 1]).then_inc(df_e, 1)
                    if 0 <= s - 3 < DS:
                        n = s - 3
                        t, rows, keep, k0, kt = DF[n]
                        act.wait_ge(df_mix, u * DS + n + 1)
                        act.wait_ge(df_sq, u * DS + max(n - 1, 0))
                        apart(act)
                        act.activation(e_sq[0:keep, n % 2, :], mix[0:keep, t, bass.ds(NA_W + u * P, P)], ACT.Square,
                                       accum_out=ms_d[0:keep, t, bass.ds(u, 1)]).then_inc(df_sq, 1)

            act.wait_ge(df_sq, DS * UNITS)

            def c_pair(i, bs, rows):
                for b in bs:
                    act.wait_ge(mT_ready, 2 * i)
                    copy(mixs[0:rows, b:b + 1, 0:NA_W], mix[0:rows, tile_of(i, b), 0:NA_W]).then_inc(mixs_a, 1)
                for b in bs:
                    act.wait_ge(x2_ready, 2 * i + b + 1)
                    act.wait_ge(rstd2_ready, 2 * i)
                    act.activation(junk2[0:rows, b, :], x2[0:rows, b, :], ACT.Square,
                                   accum_out=ms2[0:rows, b, :]).then_inc(ss2_ready, 1)
                    act.wait_ge(rstd2_ready, 2 * i + b + 1)
                    act.wait_ge(xn2_out[b], 16 * i)
                    act.wait_ge(h2_ready, 2 * i)
                    copy(xn2[0:rows, b, :], x2[0:rows, b, :], rstd[0:rows, b, :]).then_inc(xn2_ready, 1)
                for b in bs:
                    act.wait_ge(lg_max, 2 * i + b + 1)
                    act.wait_ge(affT_ready, 2 * i)
                    act.activation(lg_e[0:rows, b, :], ps[0:rows, (4 + 2 * b) * BANK:(4 + 2 * b) * BANK + N_EXP], ACT.Exp,
                                   bias=nmax[0:rows, b, 0:1], accum_out=ssum[0:rows, b, 0:1]).then_inc(lg_exp, 1)
                for b in bs:
                    act.wait_ge(affT_ready, 2 * i + b + 1)
                    off = (4 + 2 * b) * BANK + 128
                    copy(aff_all[:, bass.ds((2 * i + b) * P, rows)], ps[0:N_EXP, off:off + rows]).then_inc(affT_evac, 1)

            def tile_of(i, b):
                return bass.ds(2 * i + b, 1)

            with act.Fori(0, PAIRS) as i:
                c_pair(i, (0, 1), P)
            c_pair(PAIRS, (0,), TAIL)

            def split_hi(e, c, j):
                f = e * NCH + c
                b = c % 2
                act.wait_ge(raw_in[b][j], 16 * (e * (NCH // 2) + c // 2) + 16)
                if j == 2:
                    act.wait_ge(dn_used, f + 1)
                else:
                    act.wait_ge(gu_ready, FT * f)
                copy(w_hi[:, b, j, :], raw[:, b, j, :]).then_inc(hi_done, 1)

            def silu(e, c):
                f = e * NCH + c
                for m in range(FT):
                    n = FT * f + m
                    act.wait_ge(gu_ready, n + 1 + FT)
                    act.wait_ge(act_f, n)
                    off = (4 + m) * BANK
                    act.activation(sil[:, m, :], ps[:, off:off + SLOTS], ACT.Silu).then_inc(silu_done, 1)
                for m in range(FT):
                    n = FT * f + m
                    act.wait_ge(act_f, n + 2)
                    act.wait_ge(dn_used, f + 1)
                    copy(a_hi[:, c % 2, m, :], hf[:, m, :]).then_inc(act_hi, 1)

            def xe_hi_part(turn):
                for k in range(KD):
                    act.wait_ge(xgT_ready, turn * (KD // 2) + k // 2 + 1)
                    off = (6 + (k // 2) % 2) * BANK + (k % 2) * SLOTS
                    copy(xe_hi[:, k, :], ps[:, off:off + SLOTS], vec[:, KD + k:KD + k + 1]).then_inc(xe_hi_done, 1)

            act.sem_inc(act_hi, 1)
            xe_hi_part(0)
            with act.Fori(0, N_EXP) as e:
                for c in range(NCH):
                    split_hi(e, c, 0)
                    split_hi(e, c, 1)
                    if c >= 1:
                        silu(e, c - 1)
                    split_hi(e, c, 2)
                silu(e, NCH - 1)
                xe_hi_part(e + 1)
                for q in (0, 2):
                    act.wait_ge(y_ready, e * 3 + q + 1)
                    act.wait_ge(yt_ready, 2 * e)
                    copy(yT[:, 2 * q:2 * q + 2, :], ps[:, q * BANK:q * BANK + 2 * SLOTS]
                         .rearrange("p (j n) -> p j n", n=SLOTS)).then_inc(yT_a, 1)
                for hh in range(2):
                    act.wait_ge(yt_ready, 2 * e + hh + 1)
                    act.wait_ge(scatter_out, 32 * e)
                    act.wait_ge(gate_cp, e + 1)
                    copy(ye[:, hh, 0:512], ps[0:HS, 6 * BANK:7 * BANK], gate_cur[:, hh:hh + 1]).then_inc(ye_a, 1)

            for n in range(PAIRS):
                act.wait_ge(xf_in[n], 16)
                for b in range(2):
                    act.wait_ge(rstd3, 2 * n)
                    act.activation(junk3[:, b, :], xf[:, 2 * n + b, :], ACT.Square, accum_out=ms2[:, b, :]).then_inc(ss3, 1)

        @block.vector
        def _(dve):
            own = Chain(dve_own)

            dve.memset(half_neg[:, :], -0.5).then_inc(consts_dve, 1)
            dve.memset(mask_fill[:, :], MASKED).then_inc(fill_ready, 1)
            dve.wait_ge(const_in, 16 * 5)
            for n in range(2):
                dve.tensor_tensor_reduce(out=lam_t[:, n, :], in0=lam4[:, 2 * n, :], in1=lam4[:, 2 * n + 1, :],
                                         scale=1.0, scalar=0.0, op0=ALU.mult, op1=ALU.add,
                                         accum_out=lam_s[:, n:n + 1]).then_inc(lam_dot, 1)
            dve.wait_ge(lam_exp, 1)
            own.mark(dve.tensor_tensor(neglam[:, :], lam_e[:, 1:2], lam_e[:, 0:1], ALU.subtract))
            own.settle(dve)
            own.mark(dve.tensor_scalar(neglam[:, :], neglam[:, :], -LAMBDA_INIT, None, ALU.add))
            own.flat()

            def a_tiles(i, bs, rows):
                for b in bs:
                    dve.wait_ge(ss_ready, 2 * i + b + 1)
                    dve.tensor_scalar(ms[0:rows, b, :], ms[0:rows, b, :], 1.0 / D, RMS_EPS,
                                      ALU.mult, ALU.add).then_inc(ms_ready, 1)
                    dve.wait_ge(rstd_ready, 2 * i + b + 1)
                    dve.wait_ge(xT_ready, 2 * i)
                    dve.tensor_scalar(xn[0:rows, b, :], xt[0:rows, b, :], rstd[0:rows, b, :], None,
                                      ALU.mult).then_inc(xn_ready, 1)
                for b in bs:
                    dve.wait_ge(xT_ready, 2 * i + b + 1)
                    src = ps[:, 2 * b * BANK:(2 * b + 2) * BANK].rearrange("p (k r) -> p k r", r=P)
                    dve.tensor_tensor(hT[:, :, bass.ds((2 * i + b) * P, rows)], src[:, :, 0:rows],
                                      bcast(vec, 0, [[1, KD], [0, rows]]), ALU.mult).then_inc(h_ready, 1)

            with dve.Fori(0, PAIRS) as i:
                a_tiles(i, (0, 1), P)
            a_tiles(PAIRS, (0,), TAIL)

            dve.wait_ge(fill_in, 16 * (GRID_W * NA_HEADS * ROFF * GRID_W // (P * 960)))
            dve.memset(bias_i[64:128, :, 0:64], MASKED)
            dve.memset(bias_i[0:64, :, 528:592], MASKED).then_inc(mask_ready, 1)
            dve.memset(ms_d[:, :, :], 1.0).then_inc(mask_ready, 1)

            def evac_v(base, n0):
                for g in range(4):
                    dve.wait_ge(pj_ready, base + 8 + g + 1)
                    src = ps[:, (6 + g % 2) * BANK:(7 + g % 2) * BANK].rearrange("p (j n) -> p j n", n=P)
                    if g < 3:
                        dve.tensor_copy(v[:, 4 * g:4 * g + 4, :], src).then_inc(v_evac, 1)
                    else:
                        dve.tensor_copy(v[0:TAIL, 4 * g, :], src[0:TAIL, 0, :]).then_inc(v_evac, 1)

            def na_mix_part(u, n):
                a, t, rows, k0, ninth, _ = NA[n]
                dve.wait_ge(na_e, u * NS + n + 1)
                own.mark(dve.reciprocal(rec[0:rows, n % 4, 0:1], ssum[0:rows, n % 4, 0:1]))
                dve.wait_ge(na_o, u * NS + n + 1)
                own.settle(dve)
                off = (6 + n % 2) * BANK
                dve.tensor_scalar(mix[0:rows, t, bass.ds(u * P + a * DH, DH)], ps[0:rows, off:off + DH],
                                  rec[0:rows, n % 4, 0:1], None, ALU.mult).then_inc(na_mix, 1)

            per = NS + sum(1 for x in NA if x[3] is not None)
            with dve.Fori(0, UNITS) as u:
                own.enter(u, per)
                evac_v(u * 12, u * 4)
                dve.wait_ge(bias_in, 16 * 12 * (u + 1))
                for s in range(NS + 3):
                    if 0 <= s - 2 < NS:
                        n = s - 2
                        a, t, rows, k0, ninth, _ = NA[n]
                        dve.wait_ge(na_t, u * NS + n + 1)
                        if n >= 2:
                            dve.wait_ge(na_o, u * NS + n - 1)
                        last = dve.tensor_copy(et_na[0:N_META, n % 2, 512:512 + rows], ps[0:N_META, 5 * BANK:5 * BANK + rows])
                        if ninth is not None:
                            last = dve.tensor_copy(et_na[0:64, n % 2, 640:768], ps[0:64, 5 * BANK + P:5 * BANK + 2 * P])
                        last.then_inc(na_et_d, 1)
                    if s < NS:
                        a, t, rows, k0, ninth, r0 = NA[s]
                        dve.wait_ge(na_s, u * NS + s + 1)
                        if s >= 2:
                            dve.wait_ge(na_e, u * NS + s - 1)
                        c0 = (s % 2) * 2 * BANK

                        def add_bias(c, w, bias, init, acc):
                            return dve.tensor_tensor_reduce(
                                out=s2[0:rows, s % 2, c:c + w], in0=ps[0:rows, c0 + c:c0 + c + w], in1=bias,
                                scale=-1.0, scalar=init, op0=ALU.add, op1=ALU.min, accum_out=acc)

                        m = nmax[0:rows, s % 2, 0:1]
                        apart(dve)
                        if k0 is None:
                            add_bias(512, 16, bias_i[0:rows, a, 512:528], 3e38, m).then_inc(na_sb, 1)
                        elif ninth is not None:
                            own.mark(dve.memset(mx0[:, s % 2, :], 3e38))
                            add_bias(0, 592, bias_i[:, a, :], 3e38, m).then_inc(na_sb, 1)
                        else:
                            own.mark(add_bias(512, 16, bias_i[:, a, 512:528], 3e38, mx0[:, s % 2, :]))
                            own.settle(dve)
                            apart(dve)
                            add_bias(0, 512, bias_e[:, a, r0 - 1:r0 + 7, :].rearrange("p t k -> p (t k)"),
                                     mx0[:, s % 2, :], m).then_inc(na_sb, 1)
                    if 0 <= s - 3 < NS:
                        na_mix_part(u, s - 3)
                own.leave(UNITS)

            dper = 2 * DS
            with dve.Fori(0, UNITS) as u:
                own.enter(u, dper + 10)
                dve.wait_ge(qk_evac, 8 * u + 8 * UNITS + 8)
                dve.wait_ge(swp_in, 128 * (u + 1))
                for raw_t, swp, dst in ((q_raw, q_swp, qT), (k_raw, k_swp, kT)):
                    own.mark(dve.tensor_tensor(dst[:, :], raw_t[:, :], cos[:, :], ALU.mult))
                    own.mark(dve.tensor_tensor(swp[:, :], swp[:, :], sin[:, :], ALU.mult))
                    own.settle(dve)
                    dve.tensor_tensor(dst[:, :], dst[:, :], swp[:, :], ALU.add).then_inc(qk_rot, 1)
                evac_v(u * 12 + 12 * UNITS, u * 4 + 4 * UNITS)
                dve.wait_ge(df_ms, u + 1)
                for t0, nt, rows in ((0, FULL, P), (FULL, 1, TAIL)):
                    src = ps[0:rows, 0:2 * BANK].rearrange("p (c n) -> p c n", c=2)
                    own.mark(dve.tensor_scalar(nsm[0:rows, :, t0 * N_META:(t0 + nt) * N_META],
                                               src[:, :, t0 * N_META:(t0 + nt) * N_META], -1.0, None, ALU.mult))
                own.settle(dve)
                dve.sem_inc(df_msn, 1)
                for t0, nt, rows in ((0, FULL, P), (FULL, 1, TAIL)):
                    for c in range(2):
                        own.mark(dve.tensor_reduce(nmm[0:rows, c, t0:t0 + nt],
                                                   nsm[0:rows, c, t0 * N_META:(t0 + nt) * N_META]
                                                   .rearrange("p (t m) -> p t m", m=N_META), AX.X, ALU.min))
                own.settle(dve)
                for s in range(DS + 4):
                    if 0 <= s - 2 < DS:
                        n = s - 2
                        t, rows, keep, k0, kt = DF[n]
                        dve.wait_ge(df_t, u * DS + n + 1)
                        if n >= 2:
                            dve.wait_ge(df_o, u * DS + n - 1)
                        if kt > 4:
                            dve.tensor_copy(et_df[:, n % 2, 4 * P:8 * P].rearrange("p (j r) -> p j r", r=P)[:, :, 0:rows],
                                            ps[:, 5 * BANK:6 * BANK].rearrange("p (j r) -> p j r", r=P)[:, :, 0:rows])
                        dve.tensor_copy(et_df[0:N_META, n % 2, 8 * P:8 * P + rows],
                                        ps[0:N_META, 6 * BANK:6 * BANK + rows]).then_inc(df_et_d, 1)
                    if s < DS:
                        t, rows, keep, k0, kt = DF[s]
                        w = kt * P + N_META
                        if s >= 2:
                            dve.wait_ge(df_e, 2 * (u * DS + s - 1))
                        dve.tensor_copy(e_df[0:rows, s % 2, :, kt * P:w], nsm[0:rows, :, t * N_META:(t + 1) * N_META])
                        for c in range(2):
                            dve.wait_ge(df_s, 2 * (u * DS + s) + c + 1)
                            dve.tensor_scalar(e_df[0:rows, s % 2, c, 0:kt * P],
                                              ps[0:rows, 2 * c * BANK:2 * c * BANK + kt * P], -1.0,
                                              nmm[0:rows, c, t:t + 1], ALU.mult, ALU.min,
                                              accum_out=nmax[0:rows, s % 2, c:c + 1]).then_inc(df_m, 1)
                    if 0 <= s - 3 < DS:
                        n = s - 3
                        t, rows, keep, k0, kt = DF[n]
                        dve.wait_ge(df_o, u * DS + n + 1)
                        if n == DS - 1:
                            dve.wait_ge(df_sq, u * DS + n)
                        dve.tensor_scalar(mix[0:keep, t, bass.ds(NA_W + u * P, P)],
                                          ps[0:keep, 7 * BANK:7 * BANK + P],
                                          rec[0:keep, n % 4, 0:1], None, ALU.mult).then_inc(df_mix, 1)
                    if 0 <= s - 1 < DS:
                        n = s - 1
                        t, rows, keep, k0, kt = DF[n]
                        w = kt * P + N_META
                        b = n % 2
                        dve.wait_ge(df_e, 2 * (u * DS + n) + 2)
                        own.mark(dve.reciprocal(rec[0:rows, n % 4, :], ssum[0:rows, n % 4, :]))
                        own.settle(dve)
                        own.mark(dve.tensor_scalar(sr[0:rows, b, :], rec[0:rows, n % 4, 1:2], ssum[0:rows, n % 4, 0:1],
                                                   neglam[0:rows, :], ALU.mult, ALU.mult))
                        own.settle(dve)
                        dve.scalar_tensor_tensor(out=e_df[0:rows, b, 0, 0:w], in0=e_df[0:rows, b, 1, 0:w],
                                                 scalar=sr[0:rows, b, :], in1=e_df[0:rows, b, 0, 0:w],
                                                 op0=ALU.mult, op1=ALU.add).then_inc(df_c, 1)
                own.leave(UNITS)

            dve.wait_ge(df_sq, DS * UNITS)
            keep2 = (1.0 - LAMBDA_INIT) ** 2
            dve.tensor_scalar(ms_d[:, :, :], ms_d[:, :, :], 1.0 / (P * keep2), SUB_EPS / keep2, ALU.mult, ALU.add).then_inc(sub_ms, 1)
            own.mark(dve.memset(aff[:, :], -1.0))
            own.settle(dve)
            dve.wait_ge(sub_rstd, 1)
            own.flat()

            def c_pair(i, bs, rows):
                for b in bs:
                    dve.wait_ge(mT_ready, 2 * i)
                    t = bass.ds(2 * i + b, 1)
                    dve.tensor_tensor(mixs[0:rows, b, NA_W:D].rearrange("p (h f) -> p h f", f=P),
                                      mix[0:rows, t, NA_W:D].rearrange("p o (h f) -> p (o h) f", f=P),
                                      rstd_d[0:rows, t, :].rearrange("p o (h f) -> p (o h) f", f=1)
                                      .to_broadcast([rows, UNITS, P]),
                                      ALU.mult).then_inc(mixs_d, 1)
                for b in bs:
                    dve.wait_ge(mT_ready, 2 * i + b + 1)
                    src = ps[:, 2 * b * BANK:(2 * b + 2) * BANK].rearrange("p (k r) -> p k r", r=P)
                    dve.tensor_tensor(mixT[:, b, :, 0:rows], src[:, :, 0:rows],
                                      bcast(vec, 2 * KD, [[1, KD], [0, rows]]), ALU.mult).then_inc(mT_evac, 1)
                for b in bs:
                    dve.wait_ge(o_ready, 2 * i + b + 1)
                    dve.wait_ge(xr_in[b], 16 * i + 16)
                    dve.wait_ge(x2_out[b], 16 * i)
                    dve.wait_ge(xn2_ready, 2 * i)
                    off = (4 + 2 * b) * BANK
                    dve.tensor_tensor(x2[0:rows, b, :], ps[0:rows, off:off + D], xr[0:rows, b, :],
                                      ALU.add).then_inc(x2_ready, 1)
                    dve.wait_ge(ss2_ready, 2 * i + b + 1)
                    dve.tensor_scalar(ms2[0:rows, b, :], ms2[0:rows, b, :], 1.0 / D, RMS_EPS,
                                      ALU.mult, ALU.add).then_inc(ms2_ready, 1)
                for b in bs:
                    dve.wait_ge(h2_ready, 2 * i + b + 1)
                    dve.wait_ge(lg_ready, 2 * i)
                    src = ps[:, 2 * b * BANK:(2 * b + 2) * BANK].rearrange("p (k r) -> p k r", r=P)
                    dve.tensor_tensor(h2T[:, b, :, 0:rows], src[:, :, 0:rows],
                                      bcast(vec, KD, [[1, KD], [0, rows]]), ALU.mult).then_inc(h2_evac, 1)
                for b in bs:
                    dve.wait_ge(lg_ready, 2 * i + b + 1)
                    off = (4 + 2 * b) * BANK
                    dve.tensor_reduce(nmax[0:rows, b, 0:1], ps[0:rows, off:off + N_EXP], AX.X, ALU.max,
                                      negate=True).then_inc(lg_max, 1)
                    dve.wait_ge(lg_exp, 2 * i + b + 1)
                    own.mark(dve.reciprocal(rec[0:rows, b, 0:1], ssum[0:rows, b, 0:1]))
                    own.settle(dve)
                    dve.tensor_scalar(lg_a[0:rows, b, :], lg_e[0:rows, b, :], rec[0:rows, b, 0:1], None,
                                      ALU.mult).then_inc(lg_aff, 1)

            with dve.Fori(0, PAIRS) as i:
                own.enter(i, 2)
                c_pair(i, (0, 1), P)
                own.leave(PAIRS)
            c_pair(PAIRS, (0,), TAIL)
            own.flat()

            dve.wait_ge(affT_evac, NT)
            own.mark(dve.tensor_copy(aff[0:N_EXP, N_META:N_META + N_PROMPT], aff_all[:, 0:N_PROMPT]))
            own.mark(dve.tensor_copy(aff[32:48, N_META:N_META + N_SAMPLE], aff_all[:, N_PROMPT:N_REAL]))
            own.mark(dve.tensor_copy(aff[0:N_EXP, 0:N_META], aff_all[:, N_REAL:N_REAL + N_META]))
            own.mark(dve.tensor_copy(aff[32:48, 0:N_META], aff_all[:, N_REAL + N_META:NTOK]))
            own.settle(dve)
            for r in range(-(-CAP_P // 8)):
                top = top_v[:, 8 * r:8 * r + 8]
                own.mark(dve.max(top, aff[:, :]))
                own.settle(dve)
                own.mark(dve.max_index(top_i[:, 8 * r:8 * r + 8], top, aff[:, :]))
                own.mark(dve.match_replace(aff[:, :], top, aff[:, :], -1.0))
                own.settle(dve)
            own.mark(dve.tensor_copy(top_f[:, :], top_i[:, :]))
            own.settle(dve)
            for p0, first, meta0, cap, s0 in ((0, 0, N_REAL, CAP_P, 0), (32, N_PROMPT, N_REAL + N_META, CAP_S, CAP_P)):
                part = slice(p0, p0 + N_EXP)
                shift = first - N_META
                own.mark(dve.tensor_scalar(top_m[part, 0:cap], top_f[part, 0:cap], float(N_META),
                                           float(meta0 - shift), ALU.is_lt, ALU.mult))
                own.settle(dve)
                own.mark(dve.scalar_tensor_tensor(out=slot_r[:, s0:s0 + cap], in0=top_f[part, 0:cap],
                                                  scalar=float(shift), in1=top_m[part, 0:cap],
                                                  op0=ALU.add, op1=ALU.add))
                own.mark(dve.tensor_copy(slot_g[:, s0:s0 + cap], top_v[part, 0:cap]))
            own.settle(dve)
            dve.memset(mx0[:, 0, :], 0.0).then_inc(slots_ready, 1)
            dve.wait_ge(slotT_ready, 1)
            for hh in range(2):
                own.mark(dve.tensor_copy(idxT[:, hh, 0:N_EXP], ps[0:HS, hh * P:hh * P + N_EXP]))
                own.mark(dve.tensor_copy(gateT[:, hh, 0:N_EXP], ps[0:HS, (2 + hh) * P:(2 + hh) * P + N_EXP]))
                own.mark(dve.tensor_copy(idxT[:, hh, N_EXP:N_EXP + 1], ps[0:HS, hh * P:hh * P + 1]))
            own.settle(dve)
            dve.memset(mx0[:, 0, :], 0.0).then_inc(idx_ready, 1)
            own.flat()

            def split_lo(e, c, j):
                f = e * NCH + c
                b = c % 2
                dve.wait_ge(hi_done, 3 * f + j + 1)
                dve.tensor_tensor(w_lo[:, b, j, :], raw[:, b, j, :], w_hi[:, b, j, :].bitcast(f32),
                                  ALU.subtract).then_inc(lo_done, 1)

            def hidden(e, c):
                f = e * NCH + c
                for m in range(FT):
                    n = FT * f + m
                    dve.wait_ge(silu_done, n + 1)
                    dve.wait_ge(act_hi, n)
                    dve.wait_ge(act_lo, n)
                    off = (4 + m) * BANK + SLOTS
                    dve.tensor_tensor(hf[:, m, :], sil[:, m, :], ps[:, off:off + SLOTS], ALU.mult).then_inc(act_f, 1)
                for m in range(FT):
                    n = FT * f + m
                    dve.wait_ge(act_hi, n + 2)
                    dve.tensor_tensor(a_lo[:, c % 2, m, :], hf[:, m, :], a_hi[:, c % 2, m, :].bitcast(f32),
                                      ALU.subtract).then_inc(act_lo, 1)

            def xe_lo_part(turn):
                for k in range(KD):
                    dve.wait_ge(xe_hi_done, turn * KD + 2 * (k // 2) + 2)
                    off = (6 + (k // 2) % 2) * BANK + (k % 2) * SLOTS
                    dve.scalar_tensor_tensor(out=xe_lo[:, k, :], in0=ps[:, off:off + SLOTS],
                                             scalar=vec[:, KD + k:KD + k + 1], in1=xe_hi[:, k, :].bitcast(f32),
                                             op0=ALU.mult, op1=ALU.subtract).then_inc(xe_lo_done, 1)

            dve.sem_inc(lo_done, 6)
            dve.sem_inc(act_f, 1)
            dve.sem_inc(act_lo, 1)
            xe_lo_part(0)
            with dve.Fori(0, N_EXP) as e:
                dve.wait_ge(ye_a, 2 * e)
                dve.wait_ge(ye_d, 2 * e)
                dve.tensor_copy(gate_cur[:, :].rearrange("p (h o) -> p h o", o=1),
                                gateT[:, :, bass.ds(e, 1)]).then_inc(gate_cp, 1)
                for c in range(NCH):
                    split_lo(e, c, 0)
                    split_lo(e, c, 1)
                    if c >= 1:
                        hidden(e, c - 1)
                    split_lo(e, c, 2)
                hidden(e, NCH - 1)
                xe_lo_part(e + 1)
                for q in (1, 3):
                    if q < 3:
                        dve.wait_ge(y_ready, e * 3 + q + 1)
                    else:
                        dve.wait_ge(dn_used, NCH * (e + 1) + 2)
                    dve.wait_ge(yt_ready, 2 * e)
                    dve.tensor_copy(yT[:, 2 * q:2 * q + 2, :], ps[:, q * BANK:q * BANK + 2 * SLOTS]
                                    .rearrange("p (j n) -> p j n", n=SLOTS)).then_inc(yT_d, 1)
                for hh in range(2):
                    dve.wait_ge(yt_ready, 2 * e + hh + 1)
                    dve.wait_ge(scatter_out, 32 * e)
                    dve.wait_ge(gate_cp, e + 1)
                    dve.tensor_scalar(ye[:, hh, 512:D], ps[0:HS, 7 * BANK:8 * BANK], gate_cur[:, hh:hh + 1], None,
                                      ALU.mult).then_inc(ye_d, 1)

            dve.wait_ge(g_in, 16)
            with dve.Fori(0, PAIRS) as i:
                for b in range(2):
                    dve.wait_ge(ss3, 2 * i + b + 1)
                    dve.tensor_scalar(ms2[:, b, :], ms2[:, b, :], 1.0 / D, RMS_EPS, ALU.mult, ALU.add).then_inc(ms3, 1)
                for b in range(2):
                    dve.wait_ge(rstd3, 2 * i + b + 1)
                    dve.wait_ge(y_out[b], 16 * i)
                    dve.scalar_tensor_tensor(out=yo[:, b, :], in0=xf[:, bass.ds(2 * i + b, 1), :].rearrange("p o d -> p (o d)"),
                                             scalar=rstd[:, b, :], in1=g_fin[:, :], op0=ALU.mult,
                                             op1=ALU.mult).then_inc(y3, 1)

        @block.tensor
        def _(pe):
            pe.wait_ge(const_in, 16 * 5)

            def a_tiles(i, bs, rows):
                for b in bs:
                    pe.wait_ge(xn_ready, 2 * i + b + 1)
                    pe.wait_ge(h_ready, 2 * i)
                    for k in range(KD):
                        off = 2 * b * BANK + k * P
                        ins = pe.transpose(ps[:, off:off + rows], xn[0:rows, b, k * P:(k + 1) * P], ident[0:rows, 0:rows])
                    ins.then_inc(xT_ready, 1)

            with pe.Fori(0, PAIRS) as i:
                a_tiles(i, (0, 1), P)
            a_tiles(PAIRS, (0,), TAIL)

            def project(u, uu):
                pe.wait_ge(w_qkv_in, 48 * (uu + 1))
                pe.wait_ge(v_evac, 4 * uu)
                for n in range(8):
                    c, which = n // 2, n % 2
                    if n >= 2:
                        pe.wait_ge(qk_evac, 8 * uu + n - 1)
                    off = (6 + n % 2) * BANK
                    for k in range(KD):
                        ins = pe.matmul(ps[:, off:off + QCH], wqkv[:, k, which * P:(which + 1) * P],
                                        hT[:, k, c * QCH:(c + 1) * QCH], start=(k == 0), stop=(k == KD - 1))
                    ins.then_inc(pj_ready, 1)
                for g in range(4):
                    if g < 2:
                        pe.wait_ge(qk_evac, 8 * uu + 7 + g)
                    else:
                        pe.wait_ge(v_evac, 4 * uu + g - 1)
                    for t in range(4 * g, min(4 * g + 4, NT)):
                        rows = P if t < FULL else TAIL
                        off = (6 + g % 2) * BANK + (t - 4 * g) * P
                        for k in range(KD):
                            ins = pe.matmul(ps[0:rows, off:off + P], hT[:, k, t * P:t * P + rows],
                                            wqkv[:, k, 2 * P:3 * P], start=(k == 0), stop=(k == KD - 1))
                    ins.then_inc(pj_ready, 1)

            et_a_count = [sum(1 for x in NA[:n + 1] if x[3] is not None) for n in range(NS)]
            per_a = et_a_count[-1]
            pe.wait_ge(h_ready, NT)
            with pe.Fori(0, UNITS) as u:
                pe.wait_ge(na_mix, NS * u)
                project(u, u)
                pe.wait_ge(qk_evac, 8 * (u + 1))
                pe.wait_ge(v_evac, 4 * (u + 1))
                for s in range(NS + 2):
                    if s < NS:
                        a, t, rows, k0, ninth, _ = NA[s]
                        if s >= 2:
                            pe.wait_ge(na_sb, u * NS + s - 1)
                        if rows < P:
                            apart(pe)
                        f = slice(a * DH, a * DH + DH)
                        q = qT[f, t * P:t * P + rows]
                        c0 = (s % 2) * 2 * BANK
                        if k0 is not None:
                            pe.matmul(ps[0:rows, c0:c0 + 512], q, kT[f, k0 * P:(k0 + 4) * P], start=True, stop=True)
                        ins = pe.matmul(ps[0:rows, c0 + 512:c0 + 528], q, kT[f, N_REAL:N_REAL + N_META],
                                        start=True, stop=True)
                        if ninth is not None:
                            ins = pe.matmul(ps[0:rows, c0 + 528:c0 + 592], q, kT[f, ninth * P:ninth * P + 64],
                                            start=True, stop=True)
                        ins.then_inc(na_s, 1)
                    if 0 <= s - 1 < NS:
                        n = s - 1
                        a, t, rows, k0, ninth, _ = NA[n]
                        b = n % 2
                        pe.wait_ge(na_e, u * NS + n + 1)
                        if n >= 1:
                            pe.wait_ge(na_et_a, u * per_a + et_a_count[n - 1])
                            pe.wait_ge(na_et_d, u * NS + n)
                        if rows < P:
                            apart(pe)
                        if k0 is not None:
                            for j in range(4):
                                pe.transpose(ps[:, 4 * BANK + j * P:4 * BANK + (j + 1) * P],
                                             e_na[:, b, j * P:(j + 1) * P], ident[:, :])
                        ins = pe.transpose(ps[0:N_META, 5 * BANK:5 * BANK + rows], e_na[0:rows, b, 512:528],
                                           ident[0:rows, 0:rows])
                        if ninth is not None:
                            ins = pe.transpose(ps[0:64, 5 * BANK + P:5 * BANK + 2 * P], e_na[:, b, 528:592], ident[:, :])
                        ins.then_inc(na_t, 1)
                    if 0 <= s - 2 < NS:
                        n = s - 2
                        a, t, rows, k0, ninth, _ = NA[n]
                        b = n % 2
                        pe.wait_ge(na_et_a, u * per_a + et_a_count[n])
                        pe.wait_ge(na_et_d, u * NS + n + 1)
                        if n >= 2:
                            pe.wait_ge(na_mix, u * NS + n - 1)
                        if rows < P:
                            apart(pe)
                        o = ps[0:rows, (6 + b) * BANK:(6 + b) * BANK + DH]
                        f = slice(a * DH, a * DH + DH)
                        pairs = [(et_na[0:N_META, b, 512:512 + rows], v[0:N_META, FULL, f])]
                        if k0 is not None:
                            pairs += [(et_na[:, b, j * P:(j + 1) * P], v[:, k0 + j, f]) for j in range(4)]
                        if ninth is not None:
                            pairs += [(et_na[0:64, b, 640:768], v[0:64, ninth, f])]
                        for j, (pt, vv) in enumerate(pairs):
                            ins = pe.matmul(o, pt, vv, start=(j == 0), stop=(j == len(pairs) - 1))
                        ins.then_inc(na_o, 1)

            pe.wait_ge(na_mix, NS * UNITS)
            with pe.Fori(0, UNITS) as u:
                pe.wait_ge(df_et_d, DS * u)
                pe.wait_ge(df_mix, DS * u)
                project(u, u + UNITS)
                pe.wait_ge(qk_rot, 2 * (u + 1))
                pe.wait_ge(v_evac, 4 * (u + 1) + 4 * UNITS)
                for c in range(2):
                    for t in range(NT):
                        rows = P if t < FULL else TAIL
                        f = slice(c * DH, c * DH + DH)
                        o = c * BANK + t * N_META
                        ins = pe.matmul(ps[0:rows, o:o + N_META], qT[f, t * P:t * P + rows],
                                        kT[f, N_REAL:N_REAL + N_META], start=True, stop=True)
                ins.then_inc(df_ms, 1)
                pe.wait_ge(df_msn, u + 1)
                for s in range(DS + 2):
                    if s < DS:
                        t, rows, keep, k0, kt = DF[s]
                        for c in range(2):
                            if s >= 1:
                                pe.wait_ge(df_m, 2 * (u * DS + s - 1) + c + 1)
                            if rows < P:
                                apart(pe)
                            f = slice(c * DH, c * DH + DH)
                            q = qT[f, t * P:t * P + rows]
                            o = 2 * c * BANK
                            for j in range(kt // 4):
                                ins = pe.matmul(ps[0:rows, o + j * 512:o + (j + 1) * 512], q,
                                                kT[f, (k0 + 4 * j) * P:(k0 + 4 * j + 4) * P], start=True, stop=True)
                            ins.then_inc(df_s, 1)
                    if 0 <= s - 1 < DS:
                        n = s - 1
                        t, rows, keep, k0, kt = DF[n]
                        b = n % 2
                        pe.wait_ge(df_c, u * DS + n + 1)
                        if n >= 1:
                            pe.wait_ge(df_et_a, u * DS + n)
                            pe.wait_ge(df_et_d, u * DS + n)
                        if rows < P:
                            apart(pe)
                        for j in range(kt):
                            pe.transpose(ps[:, 4 * BANK + j * P:4 * BANK + j * P + rows],
                                         e_df[0:rows, b, 0, j * P:(j + 1) * P], ident[0:rows, 0:rows])
                        pe.transpose(ps[0:N_META, 6 * BANK:6 * BANK + rows],
                                     e_df[0:rows, b, 0, kt * P:kt * P + N_META], ident[0:rows, 0:rows]).then_inc(df_t, 1)
                    if 0 <= s - 2 < DS:
                        n = s - 2
                        t, rows, keep, k0, kt = DF[n]
                        b = n % 2
                        pe.wait_ge(df_et_a, u * DS + n + 1)
                        pe.wait_ge(df_et_d, u * DS + n + 1)
                        if n >= 1:
                            pe.wait_ge(df_mix, u * DS + n)
                        if rows < P:
                            apart(pe)
                        o = ps[0:rows, 7 * BANK:7 * BANK + P]
                        pe.matmul(o, et_df[0:N_META, b, 8 * P:8 * P + rows], v[0:N_META, FULL, :], start=True, stop=False)
                        for j in range(kt):
                            ins = pe.matmul(o, et_df[:, b, j * P:j * P + rows], v[:, k0 + j, :], start=False,
                                            stop=(j == kt - 1))
                        ins.then_inc(df_o, 1)

            pe.wait_ge(w_out_in, 32)
            pe.wait_ge(df_mix, DS * UNITS)

            def c_pair(i, bs, rows):
                for b in bs:
                    pe.wait_ge(mixs_a, 2 * i + b + 1)
                    pe.wait_ge(mixs_d, 2 * i + b + 1)
                    pe.wait_ge(h2_evac, 2 * i)
                    for k in range(KD):
                        off = 2 * b * BANK + k * P
                        ins = pe.transpose(ps[:, off:off + rows], mixs[0:rows, b, k * P:(k + 1) * P], ident[0:rows, 0:rows])
                    ins.then_inc(mT_ready, 1)
                for b in bs:
                    pe.wait_ge(mT_evac, 2 * i + b + 1)
                    pe.wait_ge(affT_evac, 2 * i)
                    for n in range(2):
                        off = (4 + 2 * b + n) * BANK
                        for k in range(KD):
                            ins = pe.matmul(ps[0:rows, off:off + 512], mixT[:, b, k, 0:rows],
                                            w_out_sb[:, k, n * 512:(n + 1) * 512], start=(k == 0), stop=(k == KD - 1))
                    ins.then_inc(o_ready, 1)
                for b in bs:
                    pe.wait_ge(xn2_ready, 2 * i + b + 1)
                    for k in range(KD):
                        off = 2 * b * BANK + k * P
                        ins = pe.transpose(ps[:, off:off + rows], xn2[0:rows, b, k * P:(k + 1) * P], ident[0:rows, 0:rows])
                    ins.then_inc(h2_ready, 1)
                for b in bs:
                    pe.wait_ge(h2_evac, 2 * i + b + 1)
                    off = (4 + 2 * b) * BANK
                    for k in range(KD):
                        ins = pe.matmul(ps[0:rows, off:off + N_EXP], h2T[:, b, k, 0:rows], w_rt[:, k, :],
                                        start=(k == 0), stop=(k == KD - 1))
                    ins.then_inc(lg_ready, 1)
                for b in bs:
                    pe.wait_ge(lg_aff, 2 * i + b + 1)
                    off = (4 + 2 * b) * BANK + 128
                    pe.transpose(ps[0:N_EXP, off:off + rows], lg_a[0:rows, b, :], ident[0:rows, 0:rows]).then_inc(affT_ready, 1)

            with pe.Fori(0, PAIRS) as i:
                c_pair(i, (0, 1), P)
            c_pair(PAIRS, (0,), TAIL)

            pe.wait_ge(slots_ready, 1)
            for n, src in enumerate((slot_r, slot_g)):
                for hh in range(2):
                    off = (2 * n + hh) * P
                    ins = pe.transpose(ps[0:HS, off:off + N_EXP], src[:, hh * HS:(hh + 1) * HS], ident[0:N_EXP, 0:N_EXP])
            ins.then_inc(slotT_ready, 1)

            def gathered_to_columns(turn, prev):
                pe.wait_ge(gather_in, 32 * (turn + 1))
                if prev is not None:
                    pe.wait_ge(ye_a, prev)
                    pe.wait_ge(ye_d, prev)
                for p in range(KD // 2):
                    if p >= 2:
                        pe.wait_ge(xe_lo_done, turn * KD + 2 * (p - 1))
                    for k in (2 * p, 2 * p + 1):
                        for hh in range(2):
                            off = (6 + p % 2) * BANK + (k % 2) * SLOTS + hh * HS
                            ins = pe.transpose(ps[:, off:off + HS], xg[:, hh, k * P:(k + 1) * P], ident[0:HS, 0:HS])
                    ins.then_inc(xgT_ready, 1)

            def up_gate(e, c):
                f = e * NCH + c
                b = c % 2
                if c == 0:
                    pe.wait_ge(xe_lo_done, KD * (e + 1))
                for m in range(FT):
                    pe.wait_ge(act_f, FT * f + m)
                    for j in range(2):
                        if m == 0:
                            pe.wait_ge(lo_done, 3 * f + j + 1 + 6)
                        out = ps[:, (4 + m) * BANK + j * SLOTS:(4 + m) * BANK + (j + 1) * SLOTS]
                        for k in range(KD):
                            cols = slice(k * FCH + m * P, k * FCH + (m + 1) * P)
                            pe.matmul(out, w_hi[:, b, j, cols], xe_hi[:, k, :], start=(k == 0), stop=False,
                                      skip_group_check=True)
                            pe.matmul(out, w_hi[:, b, j, cols], xe_lo[:, k, :], start=False, stop=False,
                                      skip_group_check=True)
                            ins = pe.matmul(out, w_lo[:, b, j, cols], xe_hi[:, k, :], start=False, stop=(k == KD - 1),
                                            skip_group_check=True)
                    ins.then_inc(gu_ready, 1)

            def down(e, c):
                f = e * NCH + c
                b = c % 2
                pe.wait_ge(lo_done, 3 * f + 3 + 6)
                pe.wait_ge(act_lo, FT * (f + 1) + 1)
                for dt in range(KD):
                    out = ps[:, (dt // 2) * BANK + (dt % 2) * SLOTS:(dt // 2) * BANK + (dt % 2 + 1) * SLOTS]
                    for m in range(FT):
                        cols = slice(m * D + dt * P, m * D + (dt + 1) * P)
                        first = c == 0 and dt % 2 == 0 and m == 0
                        last = c == NCH - 1 and m == FT - 1
                        pe.matmul(out, w_hi[:, b, 2, cols], a_hi[:, b, m, :], start=first, stop=False,
                                  skip_group_check=True)
                        pe.matmul(out, w_hi[:, b, 2, cols], a_lo[:, b, m, :], start=False, stop=False,
                                  skip_group_check=True)
                        ins = pe.matmul(out, w_lo[:, b, 2, cols], a_hi[:, b, m, :], start=False, stop=last,
                                        skip_group_check=True)
                    if c == NCH - 1 and dt in (1, 3, 5):
                        ins.then_inc(y_ready, 1)
                ins.then_inc(dn_used, 1)

            pe.sem_inc(gu_ready, FT)
            pe.sem_inc(dn_used, 2)
            gathered_to_columns(0, None)
            with pe.Fori(0, N_EXP) as e:
                for c in range(NCH):
                    up_gate(e, c)
                    if c >= 1:
                        down(e, c - 1)
                gathered_to_columns(e + 1, 2 * e)
                down(e, NCH - 1)
                for hh in range(2):
                    if hh == 0:
                        pe.wait_ge(xe_lo_done, KD * (e + 2))
                    else:
                        pe.wait_ge(ye_a, 2 * e + 1)
                        pe.wait_ge(ye_d, 2 * e + 1)
                    for k in range(KD):
                        if hh == 0 and k % 4 == 0:
                            pe.wait_ge(yT_a, 2 * e + k // 4 + 1)
                        if hh == 0 and k % 4 == 2:
                            pe.wait_ge(yT_d, 2 * e + k // 4 + 1)
                        off = 6 * BANK + k * P
                        ins = pe.transpose(ps[0:HS, off:off + P], yT[:, k, hh * HS:(hh + 1) * HS], ident[:, :])
                    ins.then_inc(yt_ready, 1)

        @block.gpsimd
        def _(pool):
            def rsqrt(out, in_, expo):
                return pool.tensor_tensor(out, in_, expo, ALU.pow)

            pool.wait_ge(consts_dve, 1)

            def stats(i, bs, rows, ready, src, done):
                for b in bs:
                    pool.wait_ge(ready, 2 * i + b + 1)
                    rsqrt(rstd[0:rows, b, :], src[0:rows, b, :], half_neg[0:rows, 0:1]).then_inc(done, 1)

            with pool.Fori(0, PAIRS) as i:
                stats(i, (0, 1), P, ms_ready, ms, rstd_ready)
            stats(PAIRS, (0,), TAIL, ms_ready, ms, rstd_ready)

            pool.wait_ge(sub_ms, 1)
            rsqrt(rstd_d[:, :, :].rearrange("p t u -> p (t u)"), ms_d[:, :, :].rearrange("p t u -> p (t u)"),
                  bcast(half_neg, 0, [[0, NT * UNITS]])).then_inc(sub_rstd, 1)

            with pool.Fori(0, PAIRS) as i:
                stats(i, (0, 1), P, ms2_ready, ms2, rstd2_ready)
            stats(PAIRS, (0,), TAIL, ms2_ready, ms2, rstd2_ready)

            pool.wait_ge(idx_ready, 1)
            for b in range(2):
                full = 16 * (PAIRS + (1 - b))
                pool.wait_ge(xn2_out[b], full)
                pool.wait_ge(x2_out[b], full)

            def gather(turn):
                pool.wait_ge(gather_in, 32 * turn)
                pool.tensor_copy(idx_gather[:, :].rearrange("p (h o) -> p h o", o=1),
                                 idxT[:, :, bass.ds(turn, 1)]).then_inc(idx_cp, 1)
                pool.wait_ge(idx_cp, turn + 1)
                apart(pool)
                for hh in range(2):
                    pool.indirect_dma_start(
                        out=xg[:, hh, :], out_offset=None, in_=h_d,
                        in_offset=bass.IndirectOffsetOnAxis(ap=idx_gather[:, hh:hh + 1], axis=0)).then_inc(gather_in, 16)

            gather(0)
            with pool.Fori(0, N_EXP) as e:
                pool.wait_ge(xgT_ready, (KD // 2) * (e + 1))
                gather(e + 1)
                pool.wait_ge(scatter_out, 32 * e)
                pool.tensor_copy(idx_scatter[:, :].rearrange("p (h o) -> p h o", o=1),
                                 idxT[:, :, bass.ds(e, 1)]).then_inc(idx_sc, 1)
                pool.wait_ge(idx_sc, e + 1)
                for hh in range(2):
                    pool.wait_ge(ye_a, 2 * e + hh + 1)
                    pool.wait_ge(ye_d, 2 * e + hh + 1)
                    apart(pool)
                    pool.indirect_dma_start(
                        out=acc_d, out_offset=bass.IndirectOffsetOnAxis(ap=idx_scatter[:, hh:hh + 1], axis=0),
                        in_=ye[:, hh, :], in_offset=None, compute_op=ALU.add).then_inc(scatter_out, 16)

            with pool.Fori(0, PAIRS) as i:
                stats(i, (0, 1), P, ms3, ms2, rstd3)


_OUT = "y_dram"


def kernel(**inputs):
    import concourse.bacc as bacc
    from concourse.bass_utils import run_bass_kernel_spmd

    a = {n: np.ascontiguousarray(x) for n, x in inputs.items()}
    nc = bacc.Bacc("TRN2", target_bir_lowering=False, num_devices=1)
    meta_pos = np.arange(N_META)
    pos = np.concatenate([N_META + np.arange(N_PROMPT), N_META + np.arange(N_SAMPLE), meta_pos, meta_pos])
    inv = np.float32(1.0) / (np.float32(10000.0) ** (np.arange(0, DH, 2, dtype=np.float32) / np.float32(DH)))
    ang = inv[:, None] * pos.astype(np.float32)[None, :]
    c, s = np.cos(ang), np.sin(ang)
    rope = np.stack([np.concatenate([c, c, c, c]), np.concatenate([-s, s, -s, s])]).astype(np.float32)
    ones = np.ones((P, KD // 2), np.float32)
    arrays = {
        "x_all": np.concatenate([a["x_prompt"][0], a["x_sample"][0], a["meta_tokens"], a["meta_tokens"]]),
        "w_in": a["w_in"][0],
        "w_out": a["w_out"][0],
        "w_router": a["w_router"][0].reshape(KD, P, N_EXP).transpose(1, 0, 2),
        "w_gate": a["w_gate"][0],
        "w_up": a["w_up"][0],
        "w_down": a["w_down"][0],
        "rpb": a["na_rpb"][0],
        "meta_bias": a["na_meta_bias"][0],
        "lambdas": np.stack([a[f"lambda_{n}"][0] for n in ("q1", "k1", "q2", "k2")]),
        "vecs": np.concatenate([a["norm_mix"][0].reshape(KD, P).T, a["norm_ffn"][0].reshape(KD, P).T, ones,
                                np.repeat(a["diff_subln"][0][:, None], KD // 2, axis=1)], axis=1),
        "final_norm": a["final_norm"],
        "rope": rope,
        "ident": np.eye(P, dtype=np.float32),
    }
    arrays = {f"{n}_dram": np.ascontiguousarray(x) for n, x in arrays.items()}
    aps = [nc.dram_tensor(n, x.shape, mybir.dt.from_np(x.dtype), kind="ExternalInput").ap() for n, x in arrays.items()]
    out = nc.dram_tensor(_OUT, (N_REAL, D), f32, kind="ExternalOutput").ap()
    build(nc, *aps, out)
    r = run_bass_kernel_spmd(nc, [arrays], core_ids=[0])
    got = r.results[0][_OUT]
    return got[None, :N_PROMPT], got[None, N_PROMPT:]
```

```python
from contextlib import ExitStack

import numpy as np

import concourse.bass as bass
from concourse import mybir

f32 = mybir.dt.float32
f32r = mybir.dt.float32r
u32 = mybir.dt.uint32
ALU = mybir.AluOpType
ACT = mybir.ActivationFunctionType
AX = mybir.AxisListType

P = 128
D = 1024
KD = D // P
N_META = 16
GRID_W = 64
DH = 64
NA_HEADS = 8
N_PROMPT, N_SAMPLE = 1024, 512
N_REAL = N_PROMPT + N_SAMPLE
FULL = N_REAL // P
TAIL = 2 * N_META
NTOK = N_REAL + TAIL
NT = FULL + 1
PT = N_PROMPT // P
NA_W = 512
PROJ = 3072
UNITS = 4
N_EXP = 16
D_FF = 2048
CAP_P = 2 * (N_PROMPT + N_META) // N_EXP
CAP_S = 2 * (N_SAMPLE + N_META) // N_EXP
SLOTS = CAP_P + CAP_S
HS = SLOTS // 2
KH, KW = 8, 16
MASKED = -1e30
RMS_EPS, SUB_EPS = 1e-6, 1e-5
LAMBDA_INIT = 0.2
QCH = NTOK // 4
FCH = 256
NF = D_FF // P
PIECE = KD * FCH
GU = 2 * D_FF // FCH
PIECES = GU + KD
NRAW, NW = 4, 6
LEAD = 4
CREDIT = 1


def na_steps():
    out = []
    for a in range(2):
        for t in range(FULL):
            first, tiles = (0, PT) if t < PT else (PT, FULL - PT)
            i = t - first
            k0 = min(max(i - 2, 0), tiles - 4)
            ninth = first + k0 + 4 if 2 <= i <= tiles - 3 else None
            out.append((a, t, P, first + k0, ninth, 2 * k0 - 2 * i + KH - 1))
        out.append((a, FULL, TAIL, None, None, 0))
    return out


def diff_steps():
    out = [(t, P, P, 0, PT) for t in range(PT)]
    out += [(t, P, P, PT, FULL - PT) for t in range(PT, FULL)]
    out += [(FULL, TAIL, TAIL, PT, FULL - PT), (FULL, TAIL, N_META, 0, PT)]
    return out


class Chain:

    def __init__(self, sem):
        self.sem, self.base, self.n, self.total = sem, 0, 0, 0

    def enter(self, i, per):
        self.per, self.base, self.n = per, self.total + i * per, 0

    def leave(self, turns):
        assert self.n == self.per, (self.n, self.per)
        self.total += turns * self.per
        self.base, self.n = self.total, 0

    def mark(self, ins):
        ins.then_inc(self.sem, 1)
        self.n += 1

    def settle(self, eng):
        eng.wait_ge(self.sem, self.base + self.n)

    def flat(self):
        self.total = self.base + self.n
        self.base, self.n = self.total, 0


def build(nc, x_all, w_in, w_out, w_router, w_gate, w_up, w_down, rpb, meta_bias, lambdas, vecs,
          final_norm, rope, ident_in, y):
    acc_d = nc.dram_tensor("residual_rows", (NTOK, D), f32, kind="Internal").ap()
    h_d = nc.dram_tensor("normed_rows", (NTOK, D), f32, kind="Internal").ap()
    ROFF = 2 * KH - 1
    COFF = 2 * KW - 1
    bias_h = nc.dram_tensor("column_bias", (GRID_W, NA_HEADS, ROFF, GRID_W), f32, kind="Internal")
    bias_d = bias_h.ap()

    ctx = ExitStack()
    with ctx:
        start = 16640
        limit = 229344
        spans = []

        def at(name, shape, off, dt=f32):
            size = int(np.prod(shape[1:])) * 4
            assert start <= off and off + size <= limit, (name, off, size)
            spans.append((off, off + size, name))
            return nc.alloc_sbuf_tensor_at(name, list(shape), dt, offset=off)

        class Region:
            def __init__(self, off):
                self.off = off

            def __call__(self, name, shape, dt=f32):
                t = at(name, shape, self.off, dt)
                self.off += (int(np.prod(shape[1:])) * 4 + 31) // 32 * 32
                return t

        R = Region(start)
        ident = R("ident", [P, P])
        vec = R("vec", [P, 3 * KD])
        lam4 = R("lam4", [P, 4, DH])
        neglam = R("neglam", [P, 1])
        lam_s = R("lam_s", [P, 2])
        lam_e = R("lam_e", [P, 2])
        lam_t = R("lam_t", [P, 2, DH])
        half_neg = R("half_neg", [P, 4])
        ms = R("ms", [P, 2, 1])
        ms2 = R("ms2", [P, 2, 1])
        rstd = R("rstd", [P, 2, 1])
        nmax = R("nmax", [P, 2, 2])
        mx0 = R("mx0", [P, 2, 1])
        ssum = R("ssum", [P, 4, 2])
        rec = R("rec", [P, 4, 2])
        gate_cur = R("gate_cur", [HS, 2])
        e_sq = R("e_sq", [P, 2, P])
        sr = R("sr", [P, 2, 1])
        idxT = R("idxT", [HS, 2, N_EXP], u32)
        gateT = R("gateT", [HS, 2, N_EXP])
        idx_gather = R("idx_gather", [HS, 2], u32)
        idx_scatter = R("idx_scatter", [HS, 2], u32)
        const_end = R.off

        R = Region(const_end)
        hT = R("hT", [P, KD, NTOK])
        mix = R("mix", [P, NT, D])
        after_mix = R.off
        wqkv = R("wqkv", [P, KD, 3 * P])
        qT = R("qT", [P, NTOK])
        kT = R("kT", [P, NTOK])
        v = R("v", [P, NT, P])
        cos = R("cos", [P, NTOK])
        sin = R("sin", [P, NTOK])
        ms_d = R("ms_d", [P, NT, UNITS])
        rstd_d = R("rstd_d", [P, NT, UNITS])
        kind_off = R.off
        R = Region(kind_off)
        bias_i = R("bias_i", [P, 2, 592])
        bias_e = R("bias_e", [P, 2, 14, GRID_W])
        s2 = R("s2", [P, 2, 592])
        e_na = R("e_na", [P, 2, 592])
        et_na = R("et_na", [P, 2, 768])
        mask_fill = R("mask_fill", [P, 960])
        R = Region(kind_off)
        q_raw = R("q_raw", [P, NTOK])
        k_raw = R("k_raw", [P, NTOK])
        q_swp = R("q_swp", [P, NTOK])
        k_swp = R("k_swp", [P, NTOK])
        e_df = R("e_df", [P, 2, 2, N_PROMPT + N_META])
        et_df = R("et_df", [P, 2, 9 * P])
        nsm = R("nsm", [P, 2, NT * N_META])
        nmm = R("nmm", [P, 2, NT])
        R = Region(after_mix)
        xt = R("xt", [P, 2, D])
        xn = R("xn", [P, 2, D])
        junk = R("junk", [P, 2, D])

        R = Region(const_end)
        w_out_sb = R("w_out_sb", [P, KD, D])
        w_rt = R("w_rt", [P, KD, N_EXP])
        assert R.off <= const_end + KD * NTOK * 4
        R = Region(kind_off)
        mixs = R("mixs", [P, 2, D])
        mixT = R("mixT", [P, 2, KD, P])
        xr = R("xr", [P, 2, D])
        x2 = R("x2", [P, 2, D])
        xn2 = R("xn2", [P, 2, D])
        h2T = R("h2T", [P, 2, KD, P])
        aff_end = R.off
        R = Region(after_mix)
        aff_all = R("aff_all", [N_EXP, NTOK])
        aff = R("aff", [48, N_PROMPT + N_META])
        junk2 = R("junk2", [P, 2, D])
        lg_e = R("lg_e", [P, 2, N_EXP])
        lg_a = R("lg_a", [P, 2, N_EXP])
        top_v = R("top_v", [48, 136])
        top_i = R("top_i", [48, 136], u32)
        top_f = R("top_f", [48, 136])
        top_m = R("top_m", [48, 136])
        slot_r = R("slot_r", [N_EXP, SLOTS])
        slot_g = R("slot_g", [N_EXP, SLOTS])
        assert R.off <= kind_off - 2 * NT * UNITS * 4 - 64

        R = Region(const_end)
        raw = R("raw", [P, NRAW, PIECE])
        w_hi = R("w_hi", [P, NW, PIECE], f32r)
        w_lo = R("w_lo", [P, NW, PIECE], f32r)
        xg = R("xg", [HS, 2, D])
        xe = R("xe", [P, KD, 2, SLOTS], f32r)
        hid = R("hid", [P, NF, 2, SLOTS], f32r)
        part = R("part", [P, 2, 2, SLOTS])
        gusum = R("gusum", [P, 2, 2, SLOTS])
        sil = R("sil", [P, 2, SLOTS])
        hf = R("hf", [P, 2, SLOTS])
        y_part = R("y_part", [P, 2, SLOTS])
        yT = R("yT", [P, KD, SLOTS])
        ye = R("ye", [HS, 2, D])
        R = Region(const_end)
        g_fin = R("g_fin", [P, D])
        xf = R("xf", [P, FULL, D])
        yo = R("yo", [P, 2, D])
        junk3 = R("junk3", [P, 2, D])

        ps = ctx.enter_context(nc.psum_tensor("ps", [P, 8 * 512], f32))
        BANK = 512

        def sem(name):
            return ctx.enter_context(nc.semaphore(name))

        dve_own, act_own = sem("dve_own"), sem("act_own")
        const_in = sem("const_in")
        consts_dve = sem("consts_dve")
        lam_dot, lam_exp = sem("lam_dot"), sem("lam_exp")
        x_in = [sem(f"x_in{b}") for b in range(2)]
        ss_ready, ms_ready, rstd_ready = sem("ss_ready"), sem("ms_ready"), sem("rstd_ready")
        xn_ready, xT_ready, h_ready = sem("xn_ready"), sem("xT_ready"), sem("h_ready")
        w_qkv_in, pj_ready = sem("w_qkv_in"), sem("pj_ready")
        qk_evac, v_evac = sem("qk_evac"), sem("v_evac")
        fill_ready, fill_in, diag_in = sem("fill_ready"), sem("fill_in"), sem("diag_in")
        mask_ready, bias_in = sem("mask_ready"), sem("bias_in")
        na_s, na_sb, na_e, na_t = sem("na_s"), sem("na_sb"), sem("na_e"), sem("na_t")
        na_et_a, na_et_d, na_o, na_mix = sem("na_et_a"), sem("na_et_d"), sem("na_o"), sem("na_mix")
        swp_in, qk_rot = sem("swp_in"), sem("qk_rot")
        df_ms, df_msn = sem("df_ms"), sem("df_msn")
        df_s, df_m, df_e, df_c = sem("df_s"), sem("df_m"), sem("df_e"), sem("df_c")
        df_t, df_et_a, df_et_d = sem("df_t"), sem("df_et_a"), sem("df_et_d")
        df_o, df_mix, df_sq = sem("df_o"), sem("df_mix"), sem("df_sq")
        w_out_in, sub_ms, sub_rstd = sem("w_out_in"), sem("sub_ms"), sem("sub_rstd")
        mixs_a, mixs_d, mT_ready, mT_evac = sem("mixs_a"), sem("mixs_d"), sem("mT_ready"), sem("mT_evac")
        xr_in = [sem(f"xr_in{b}") for b in range(2)]
        o_ready, x2_ready = sem("o_ready"), sem("x2_ready")
        x2_out = [sem(f"x2_out{b}") for b in range(2)]
        xn2_out = [sem(f"xn2_out{b}") for b in range(2)]
        ss2_ready, ms2_ready, rstd2_ready = sem("ss2_ready"), sem("ms2_ready"), sem("rstd2_ready")
        xn2_ready, h2_ready, h2_evac = sem("xn2_ready"), sem("h2_ready"), sem("h2_evac")
        lg_ready, lg_max, lg_exp, lg_aff = sem("lg_ready"), sem("lg_max"), sem("lg_exp"), sem("lg_aff")
        affT_ready, affT_evac = sem("affT_ready"), sem("affT_evac")
        slots_ready, slotT_ready, idx_ready = sem("slots_ready"), sem("slotT_ready"), sem("idx_ready")
        raw_in = [sem(f"raw_in{b}") for b in range(NRAW)]
        hi_done, lo_done = sem("hi_done"), sem("lo_done")
        idx_cp, gather_in = sem("idx_cp"), sem("gather_in")
        xgT_ready, xe_hi_done, xe_lo_done = sem("xgT_ready"), sem("xe_hi_done"), sem("xe_lo_done")
        gu_ready, part_done, sum_done, silu_done = sem("gu_ready"), sem("part_done"), sem("sum_done"), sem("silu_done")
        hf_done, hid_hi, hid_lo = sem("hf_done"), sem("hid_hi"), sem("hid_lo")
        dn_ready, ypart_done, yT_done, yt_ready = sem("dn_ready"), sem("ypart_done"), sem("yT_done"), sem("yt_ready")
        ye_a, ye_d, gate_cp = sem("ye_a"), sem("ye_d"), sem("gate_cp")
        idx_sc, scatter_out, added = sem("idx_sc"), sem("scatter_out"), sem("added")
        g_in = sem("g_in")
        xf_in = [sem(f"xf_in{n}") for n in range(FULL // 2)]
        ss3, ms3, rstd3, y3 = sem("ss3"), sem("ms3"), sem("rstd3"), sem("y3")
        y_out = [sem(f"y_out{b}") for b in range(2)]

        block = ctx.enter_context(nc.Block())

        passed = {e.engine: sem(f"passed_{n}") for n, e in
                  (("act", nc.scalar), ("dve", nc.vector), ("pe", nc.tensor), ("pool", nc.gpsimd))}

        def freed(eng, e, n):
            if n < NW:
                eng.wait_ge(dn_ready, KD * e + n + PIECES - NW - GU + 1)
            elif n < GU + NW:
                eng.wait_ge(gu_ready, NF * e + 2 * ((n - NW) // 2) + 2)
            else:
                eng.wait_ge(dn_ready, KD * e + n - NW - GU + 1 + KD)

        def apart(eng):
            eng.sem_inc(passed[eng.engine], 1)

        NA = na_steps()
        DF = diff_steps()
        NS, DS = len(NA), len(DF)
        PAIRS = FULL // 2
        w_in_v = w_in.rearrange("(k p) n -> p k n", p=P)
        w_out_v = w_out.rearrange("(k p) n -> p k n", p=P)

        def bcast(handle, off, dims):
            row = int(np.prod(handle.shape[1:]))
            return bass.AP(tensor=handle, offset=off, ap=[[row, handle.shape[0]]] + dims)

        @block.sync
        def _(sp):
            for b in range(2):
                for done in (x2_out[b], xn2_out[b], y_out[b]):
                    sp.sem_inc(done, CREDIT)
            sp.dma_start(ident[:, :], ident_in).then_inc(const_in, 16)
            sp.dma_start(vec[:, :], vecs).then_inc(const_in, 16)
            sp.dma_start(lam4[:, :, :], lambdas.partition_broadcast(P)).then_inc(const_in, 16)
            sp.dma_start(cos[:, :], rope[0]).then_inc(const_in, 16)
            sp.dma_start(sin[:, :], rope[1]).then_inc(const_in, 16)

            with sp.Fori(0, PAIRS) as i:
                for b in range(2):
                    sp.wait_ge(xn_ready, 2 * i + CREDIT)
                    sp.dma_start(xt[:, b, :], x_all[bass.ds((2 * i + b) * P, P), :]).then_inc(x_in[b], 16)
            sp.wait_ge(xn_ready, 2 * PAIRS + CREDIT)
            sp.dma_start(xt[0:TAIL, 0, :], x_all[N_REAL:NTOK, :]).then_inc(x_in[0], 16)

            flat = GRID_W * NA_HEADS * ROFF * GRID_W
            sp.wait_ge(fill_ready, 1)
            for n in range(flat // (P * 960)):
                dst = bass.AP(tensor=bias_h, offset=n * P * 960, ap=[[960, P], [1, 960]])
                sp.dma_start(dst, mask_fill[:, :]).then_inc(fill_in, 16)
            sp.wait_ge(fill_in, 16 * (flat // (P * 960)))
            row = NA_HEADS * ROFF * GRID_W
            hr = NA_HEADS * ROFF
            last_ws = GRID_W - KW
            mid0, mid1 = KW // 2, last_ws + KW // 2
            runs = [(c, 1, 0) for c in range(mid0)] + [(mid0, mid1 - mid0 + 1, 0)]
            runs += [(c, 1, last_ws) for c in range(mid1 + 1, GRID_W)]
            for c, n, ws in runs:
                first_off = ws - c + KW - 1
                src = bass.AP(tensor=rpb.tensor, offset=first_off, ap=[[COFF, hr], [1, KW]])
                dst = bass.AP(tensor=bias_h, offset=c * row + ws, ap=[[GRID_W, hr], [1, KW]])
                if n > 1:
                    src = bass.AP(tensor=rpb.tensor, offset=first_off, ap=[[0, n], [COFF, hr], [1, KW]])
                    dst = bass.AP(tensor=bias_h, offset=c * row + ws, ap=[[row + 1, n], [GRID_W, hr], [1, KW]])
                sp.dma_start(dst, src).then_inc(diag_in, 16)
            sp.wait_ge(diag_in, 16 * len(runs))

            sp.wait_ge(mask_ready, 1)
            with sp.Fori(0, UNITS) as u:
                sp.wait_ge(pj_ready, 12 * u + CREDIT)
                for j in range(3):
                    sp.dma_start(wqkv[:, :, j * P:(j + 1) * P],
                                 w_in_v[:, :, bass.ds(j * NA_W + u * P, P)]).then_inc(w_qkv_in, 16)
                sp.wait_ge(na_sb, NS * u + CREDIT)
                for a in range(2):
                    h = bass.ds(2 * u + a, 1)
                    lo, up = bias_d[:, h, :, :], bias_d[:, h, :, :]
                    for dst, src in (
                        (bias_e[0:64, a, :, :], lo[:, :, 1:15, :]),
                        (bias_e[64:128, a, :, :], up[:, :, 0:14, :]),
                        (bias_i[0:64, a, 0:512].rearrange("p (t k) -> p t k", k=GRID_W), lo[:, :, 3:11, :]),
                        (bias_i[64:128, a, 64:512].rearrange("p (t k) -> p t k", k=GRID_W), up[:, :, 3:10, :]),
                        (bias_i[64:128, a, 528:592].rearrange("p (t k) -> p t k", k=GRID_W), up[:, :, 10:11, :]),
                    ):
                        sp.dma_start(dst, src.rearrange("c h t k -> c (h t) k")).then_inc(bias_in, 16)
                    sp.dma_start(bias_i[:, a, 512:528],
                                 meta_bias[h, :].rearrange("a m -> (a m)").partition_broadcast(P)).then_inc(bias_in, 16)
            with sp.Fori(0, UNITS) as u:
                sp.wait_ge(pj_ready, 12 * u + 12 * UNITS + CREDIT)
                for j in range(3):
                    sp.dma_start(wqkv[:, :, j * P:(j + 1) * P],
                                 w_in_v[:, :, bass.ds(3 * NA_W + j * NA_W + u * P, P)]).then_inc(w_qkv_in, 16)
                sp.wait_ge(qk_evac, 8 * u + 8 * UNITS + 8)
                for src, dst in ((q_raw, q_swp), (k_raw, k_swp)):
                    for g in range(4):
                        o = g ^ 1
                        sp.dma_start(dst[32 * g:32 * g + 32, :], src[32 * o:32 * o + 32, :]).then_inc(swp_in, 16)

            sp.wait_ge(pj_ready, 12 * 2 * UNITS + CREDIT)
            sp.dma_start(w_out_sb[:, :, :], w_out_v).then_inc(w_out_in, 16)
            sp.dma_start(w_rt[:, :, :], w_router).then_inc(w_out_in, 16)
            sp.wait_ge(df_sq, DS * UNITS + CREDIT)
            with sp.Fori(0, PAIRS) as i:
                for b in range(2):
                    sp.wait_ge(x2_ready, 2 * i + CREDIT)
                    sp.dma_start(xr[:, b, :], x_all[bass.ds((2 * i + b) * P, P), :]).then_inc(xr_in[b], 16)
                for b in range(2):
                    sp.wait_ge(x2_ready, 2 * i + b + 1 + CREDIT)
                    sp.dma_start(acc_d[bass.ds((2 * i + b) * P, P), :], x2[:, b, :]).then_inc(x2_out[b], 16)
                for b in range(2):
                    sp.wait_ge(xn2_ready, 2 * i + b + 1 + CREDIT)
                    sp.dma_start(h_d[bass.ds((2 * i + b) * P, P), :], xn2[:, b, :]).then_inc(xn2_out[b], 16)
            sp.dma_start(xr[0:TAIL, 0, :], x_all[N_REAL:NTOK, :]).then_inc(xr_in[0], 16)
            sp.wait_ge(x2_ready, FULL + 1 + CREDIT)
            sp.dma_start(acc_d[N_REAL:NTOK, :], x2[0:TAIL, 0, :]).then_inc(x2_out[0], 16)
            sp.wait_ge(xn2_ready, FULL + 1 + CREDIT)
            sp.dma_start(h_d[N_REAL:NTOK, :], xn2[0:TAIL, 0, :]).then_inc(xn2_out[0], 16)

            sp.wait_ge(lg_ready, NT + CREDIT)
            with sp.Fori(0, N_EXP) as e:
                one = bass.ds(e, 1)
                for n in range(PIECES):
                    sp.wait_ge(lo_done, PIECES * e + n + 1)
                    if n < GU:
                        c = n // 2
                        src = (w_gate, w_up)[n % 2][one, :, c * FCH:(c + 1) * FCH].rearrange("o (k p) f -> p (o k) f", p=P)
                        dst = raw[:, n % NRAW, :].rearrange("p (k f) -> p k f", f=FCH)
                    else:
                        c = n - GU
                        src = w_down[one, :, c * P:(c + 1) * P].rearrange("o (m p) n -> p (o m) n", p=P)
                        dst = raw[:, n % NRAW, :].rearrange("p (m n) -> p m n", n=P)
                    sp.dma_start(dst, src).then_inc(raw_in[n % NRAW], 16)

            sp.wait_ge(added, N_EXP + 1)
            sp.dma_start(g_fin[:, :], final_norm.partition_broadcast(P)).then_inc(g_in, 16)
            for n in range(PAIRS):
                sp.dma_start(xf[:, 2 * n:2 * n + 2, :],
                             acc_d[2 * n * P:(2 * n + 2) * P, :].rearrange("(t p) d -> p t d", p=P)).then_inc(xf_in[n], 16)
            with sp.Fori(0, PAIRS) as i:
                for b in range(2):
                    sp.wait_ge(y3, 2 * i + b + 1)
                    sp.dma_start(y[bass.ds((2 * i + b) * P, P), :], yo[:, b, :]).then_inc(y_out[b], 16)
            for b in range(2):
                sp.wait_ge(y_out[b], 16 * PAIRS + CREDIT)

        @block.scalar
        def _(act):
            own = Chain(act_own)

            def copy(out, in_, scale=1.0):
                return act.activation(out, in_, ACT.Copy, scale=scale)

            for started in (df_sq, xn2_ready, affT_evac):
                act.sem_inc(started, CREDIT)
            act.wait_ge(lam_dot, 2)
            act.activation(lam_e[:, :], lam_s[:, :], ACT.Exp).then_inc(lam_exp, 1)

            def a_tile(b, count, rows):
                act.wait_ge(x_in[b], count)
                act.activation(junk[0:rows, b, :], xt[0:rows, b, :], ACT.Square,
                               accum_out=ms[0:rows, b, :]).then_inc(ss_ready, 1)

            with act.Fori(0, PAIRS) as i:
                for b in range(2):
                    act.wait_ge(rstd_ready, 2 * i + CREDIT)
                    a_tile(b, 16 * i + 16, P)
            act.wait_ge(rstd_ready, 2 * PAIRS + CREDIT)
            a_tile(0, 16 * PAIRS + 16, TAIL)

            def evac_qk(base, q_dst, k_dst):
                for n in range(8):
                    c, which = n // 2, n % 2
                    act.wait_ge(pj_ready, base + n + 1 + CREDIT)
                    src = ps[:, (6 + n % 2) * BANK:(6 + n % 2) * BANK + QCH]
                    dst = (q_dst, k_dst)[which]
                    copy(dst[:, c * QCH:(c + 1) * QCH], src, DH ** -0.5 if which == 0 else 1.0).then_inc(qk_evac, 1)

            with act.Fori(0, UNITS) as u:
                evac_qk(u * 12, qT, kT)
                for s in range(NS + 2):
                    if s >= 2:
                        n = s - 2
                        a, t, rows, k0, ninth, _ = NA[n]
                        act.wait_ge(na_t, u * NS + n + 1)
                        if n >= 2:
                            act.wait_ge(na_o, u * NS + n - 1)
                        if k0 is not None:
                            copy(et_na[:, n % 2, 0:512], ps[:, 4 * BANK:5 * BANK]).then_inc(na_et_a, 1)
                    if s < NS:
                        a, t, rows, k0, ninth, _ = NA[s]
                        act.wait_ge(na_sb, u * NS + s + 1 + CREDIT)
                        if s >= 2:
                            act.wait_ge(na_t, u * NS + s - 1)
                        if s >= 4:
                            act.wait_ge(na_mix, u * NS + s - 3 + CREDIT)
                        cols = slice(512, 528) if k0 is None else slice(0, 592 if ninth is not None else 528)
                        act.activation(e_na[0:rows, s % 2, cols], s2[0:rows, s % 2, cols], ACT.Exp,
                                       bias=nmax[0:rows, s % 2, 0:1], scale=-1.0,
                                       accum_out=ssum[0:rows, s % 4, 0:1]).then_inc(na_e, 1)

            with act.Fori(0, UNITS) as u:
                act.wait_ge(na_mix, NS * UNITS + CREDIT)
                act.wait_ge(qk_rot, 2 * u)
                evac_qk(u * 12 + 12 * UNITS, q_raw, k_raw)
                for s in range(DS + 3):
                    if 0 <= s - 2 < DS:
                        n = s - 2
                        t, rows, keep, k0, kt = DF[n]
                        act.wait_ge(df_t, u * DS + n + 1)
                        if n >= 2:
                            act.wait_ge(df_o, u * DS + n - 1)
                        copy(et_df[:, n % 2, 0:4 * P].rearrange("p (j r) -> p j r", r=P)[:, :, 0:rows],
                             ps[:, 4 * BANK:5 * BANK].rearrange("p (j r) -> p j r", r=P)[:, :, 0:rows]).then_inc(df_et_a, 1)
                    if s < DS:
                        t, rows, keep, k0, kt = DF[s]
                        w = kt * P + N_META
                        if s >= 2:
                            act.wait_ge(df_t, u * DS + s - 1)
                        for c in range(2):
                            act.wait_ge(df_m, 2 * (u * DS + s) + c + 1)
                            act.activation(e_df[0:rows, s % 2, c, 0:w], e_df[0:rows, s % 2, c, 0:w],
                                           ACT.Exp, bias=nmax[0:rows, s % 2, c:c + 1], scale=-1.0,
                                           accum_out=ssum[0:rows, s % 4, c:c + 1]).then_inc(df_e, 1)
                    if 0 <= s - 3 < DS:
                        n = s - 3
                        t, rows, keep, k0, kt = DF[n]
                        act.wait_ge(df_mix, u * DS + n + 1 + CREDIT)
                        act.wait_ge(df_sq, u * DS + max(n - 1, 0) + CREDIT)
                        apart(act)
                        act.activation(e_sq[0:keep, n % 2, :], mix[0:keep, t, bass.ds(NA_W + u * P, P)], ACT.Square,
                                       accum_out=ms_d[0:keep, t, bass.ds(u, 1)]).then_inc(df_sq, 1)

            act.wait_ge(df_sq, DS * UNITS + CREDIT)

            def c_pair(i, bs, rows):
                for b in bs:
                    act.wait_ge(mT_ready, 2 * i + CREDIT)
                    copy(mixs[0:rows, b:b + 1, 0:NA_W], mix[0:rows, tile_of(i, b), 0:NA_W]).then_inc(mixs_a, 1)
                for b in bs:
                    act.wait_ge(x2_ready, 2 * i + b + 1 + CREDIT)
                    act.wait_ge(rstd2_ready, 2 * i + CREDIT)
                    act.activation(junk2[0:rows, b, :], x2[0:rows, b, :], ACT.Square,
                                   accum_out=ms2[0:rows, b, :]).then_inc(ss2_ready, 1)
                    act.wait_ge(rstd2_ready, 2 * i + b + 1 + CREDIT)
                    act.wait_ge(xn2_out[b], 16 * i + CREDIT)
                    act.wait_ge(h2_ready, 2 * i + CREDIT)
                    copy(xn2[0:rows, b, :], x2[0:rows, b, :], rstd[0:rows, b, :]).then_inc(xn2_ready, 1)
                for b in bs:
                    act.wait_ge(lg_max, 2 * i + b + 1)
                    act.wait_ge(affT_ready, 2 * i + CREDIT)
                    act.activation(lg_e[0:rows, b, :], ps[0:rows, (4 + 2 * b) * BANK:(4 + 2 * b) * BANK + N_EXP], ACT.Exp,
                                   bias=nmax[0:rows, b, 0:1], accum_out=ssum[0:rows, b, 0:1]).then_inc(lg_exp, 1)
                for b in bs:
                    act.wait_ge(affT_ready, 2 * i + b + 1 + CREDIT)
                    off = (4 + 2 * b) * BANK + 128
                    copy(aff_all[:, bass.ds((2 * i + b) * P, rows)], ps[0:N_EXP, off:off + rows]).then_inc(affT_evac, 1)

            def tile_of(i, b):
                return bass.ds(2 * i + b, 1)

            with act.Fori(0, PAIRS) as i:
                c_pair(i, (0, 1), P)
            c_pair(PAIRS, (0,), TAIL)

            def split_hi(e, n):
                e, n = (e + 1, n - PIECES) if n >= PIECES else (e, n)
                act.wait_ge(raw_in[n % NRAW], 16 * (e * (PIECES // NRAW) + n // NRAW) + 16)
                freed(act, e, n)
                copy(w_hi[:, n % NW, :], raw[:, n % NRAW, :]).then_inc(hi_done, 1)

            def hidden_hi(e, m):
                i = NF * e + m
                act.wait_ge(hf_done, i + 1)
                act.wait_ge(dn_ready, KD * e + KD)
                copy(hid[:, m, 0, :], hf[:, m % 2, :]).then_inc(hid_hi, 1)

            def xe_hi_part(turn):
                for k in range(KD):
                    act.wait_ge(xgT_ready, turn * (KD // 2) + k // 2 + 1)
                    off = (k // 2) * BANK + (k % 2) * SLOTS
                    copy(xe[:, k, 0, :], ps[:, off:off + SLOTS], vec[:, KD + k:KD + k + 1]).then_inc(xe_hi_done, 1)

            def result_rows(e, half):
                act.wait_ge(yt_ready, 2 * e + half + 1)
                act.wait_ge(added, e + 1)
                act.wait_ge(gate_cp, e + 1)
                copy(ye[:, 0, half * 512:(half + 1) * 512], ps[0:HS, 6 * BANK:7 * BANK],
                     gate_cur[:, 0:1]).then_inc(ye_a, 1)

            def expert(e, last):
                for m in range(NF):
                    i = NF * e + m
                    act.wait_ge(gu_ready, i + 1)
                    act.wait_ge(sum_done, i + CREDIT)
                    src = ps[:, 2 * (m % 2) * BANK:2 * (m % 2 + 1) * BANK].rearrange("p (j n) -> p j n", j=2)
                    copy(part[:, m % 2, :, :], src[:, :, SLOTS:2 * SLOTS]).then_inc(part_done, 1)
                    if m > 0:
                        hidden_hi(e, m - 1)
                    if m < NF - 1:
                        split_hi(e, m + LEAD)
                    act.wait_ge(sum_done, i + 2 + CREDIT)
                    act.activation(sil[:, m % 2, :], gusum[:, m % 2, 0, :], ACT.Silu).then_inc(silu_done, 1)
                hidden_hi(e, NF - 1)
                split_hi(e, NF - 1 + LEAD)
                for d in range(KD):
                    i = KD * e + d
                    if not last or d < KD - LEAD:
                        split_hi(e, GU + d + LEAD)
                    if d == 4 and not last:
                        xe_hi_part(e + 1)
                    if d == 5:
                        result_rows(e, 0)
                    act.wait_ge(dn_ready, i + 1 + KD)
                    act.wait_ge(yT_done, i + CREDIT)
                    off = (4 + d % 2) * BANK + SLOTS
                    copy(y_part[:, d % 2, :], ps[:, off:off + SLOTS]).then_inc(ypart_done, 1)
                result_rows(e, 1)

            act.sem_inc(ye_a, 1)
            for n in range(LEAD):
                split_hi(0, n)
            xe_hi_part(0)
            with act.Fori(0, N_EXP - 1) as e:
                expert(e, False)
            expert(N_EXP - 1, True)

            for n in range(PAIRS):
                act.wait_ge(xf_in[n], 16)
                for b in range(2):
                    act.wait_ge(rstd3, 2 * n + CREDIT)
                    act.activation(junk3[:, b, :], xf[:, 2 * n + b, :], ACT.Square, accum_out=ms2[:, b, :]).then_inc(ss3, 1)

        @block.vector
        def _(dve):
            own = Chain(dve_own)

            for started in (xn_ready, h_ready, v_evac, na_sb, na_mix, df_et_d, df_mix, x2_ready, h2_evac, sum_done,
                            yT_done):
                dve.sem_inc(started, CREDIT)
            dve.memset(half_neg[:, :], -0.5).then_inc(consts_dve, 1)
            dve.memset(mask_fill[:, :], MASKED).then_inc(fill_ready, 1)
            dve.wait_ge(const_in, 16 * 5)
            for n in range(2):
                dve.tensor_tensor_reduce(out=lam_t[:, n, :], in0=lam4[:, 2 * n, :], in1=lam4[:, 2 * n + 1, :],
                                         scale=1.0, scalar=0.0, op0=ALU.mult, op1=ALU.add,
                                         accum_out=lam_s[:, n:n + 1]).then_inc(lam_dot, 1)
            dve.wait_ge(lam_exp, 1)
            own.mark(dve.tensor_tensor(neglam[:, :], lam_e[:, 1:2], lam_e[:, 0:1], ALU.subtract))
            own.settle(dve)
            own.mark(dve.tensor_scalar(neglam[:, :], neglam[:, :], -LAMBDA_INIT, None, ALU.add))
            own.flat()

            def a_tiles(i, bs, rows):
                for b in bs:
                    dve.wait_ge(ss_ready, 2 * i + b + 1)
                    dve.tensor_scalar(ms[0:rows, b, :], ms[0:rows, b, :], 1.0 / D, RMS_EPS,
                                      ALU.mult, ALU.add).then_inc(ms_ready, 1)
                    dve.wait_ge(rstd_ready, 2 * i + b + 1 + CREDIT)
                    dve.wait_ge(xT_ready, 2 * i + CREDIT)
                    dve.tensor_scalar(xn[0:rows, b, :], xt[0:rows, b, :], rstd[0:rows, b, :], None,
                                      ALU.mult).then_inc(xn_ready, 1)
                for b in bs:
                    dve.wait_ge(xT_ready, 2 * i + b + 1 + CREDIT)
                    src = ps[:, 2 * b * BANK:(2 * b + 2) * BANK].rearrange("p (k r) -> p k r", r=P)
                    dve.tensor_tensor(hT[:, :, bass.ds((2 * i + b) * P, rows)], src[:, :, 0:rows],
                                      bcast(vec, 0, [[1, KD], [0, rows]]), ALU.mult).then_inc(h_ready, 1)

            with dve.Fori(0, PAIRS) as i:
                a_tiles(i, (0, 1), P)
            a_tiles(PAIRS, (0,), TAIL)

            dve.wait_ge(fill_in, 16 * (GRID_W * NA_HEADS * ROFF * GRID_W // (P * 960)))
            dve.memset(bias_i[64:128, :, 0:64], MASKED)
            dve.memset(bias_i[0:64, :, 528:592], MASKED).then_inc(mask_ready, 1)
            dve.memset(ms_d[:, :, :], 1.0).then_inc(mask_ready, 1)

            def evac_v(base, n0):
                for g in range(4):
                    dve.wait_ge(pj_ready, base + 8 + g + 1 + CREDIT)
                    src = ps[:, (6 + g % 2) * BANK:(7 + g % 2) * BANK].rearrange("p (j n) -> p j n", n=P)
                    if g < 3:
                        dve.tensor_copy(v[:, 4 * g:4 * g + 4, :], src).then_inc(v_evac, 1)
                    else:
                        dve.tensor_copy(v[0:TAIL, 4 * g, :], src[0:TAIL, 0, :]).then_inc(v_evac, 1)

            def na_mix_part(u, n):
                a, t, rows, k0, ninth, _ = NA[n]
                dve.wait_ge(na_e, u * NS + n + 1)
                own.mark(dve.reciprocal(rec[0:rows, n % 4, 0:1], ssum[0:rows, n % 4, 0:1]))
                dve.wait_ge(na_o, u * NS + n + 1)
                own.settle(dve)
                off = (6 + n % 2) * BANK
                dve.tensor_scalar(mix[0:rows, t, bass.ds(u * P + a * DH, DH)], ps[0:rows, off:off + DH],
                                  rec[0:rows, n % 4, 0:1], None, ALU.mult).then_inc(na_mix, 1)

            per = NS + sum(1 for x in NA if x[3] is not None)
            with dve.Fori(0, UNITS) as u:
                own.enter(u, per)
                evac_v(u * 12, u * 4)
                dve.wait_ge(bias_in, 16 * 12 * (u + 1))
                for s in range(NS + 3):
                    if 0 <= s - 2 < NS:
                        n = s - 2
                        a, t, rows, k0, ninth, _ = NA[n]
                        dve.wait_ge(na_t, u * NS + n + 1)
                        if n >= 2:
                            dve.wait_ge(na_o, u * NS + n - 1)
                        last = dve.tensor_copy(et_na[0:N_META, n % 2, 512:512 + rows], ps[0:N_META, 5 * BANK:5 * BANK + rows])
                        if ninth is not None:
                            last = dve.tensor_copy(et_na[0:64, n % 2, 640:768], ps[0:64, 5 * BANK + P:5 * BANK + 2 * P])
                        last.then_inc(na_et_d, 1)
                    if s < NS:
                        a, t, rows, k0, ninth, r0 = NA[s]
                        dve.wait_ge(na_s, u * NS + s + 1)
                        if s >= 2:
                            dve.wait_ge(na_e, u * NS + s - 1)
                        c0 = (s % 2) * 2 * BANK

                        def add_bias(c, w, bias, init, acc):
                            return dve.tensor_tensor_reduce(
                                out=s2[0:rows, s % 2, c:c + w], in0=ps[0:rows, c0 + c:c0 + c + w], in1=bias,
                                scale=-1.0, scalar=init, op0=ALU.add, op1=ALU.min, accum_out=acc)

                        m = nmax[0:rows, s % 2, 0:1]
                        apart(dve)
                        if k0 is None:
                            add_bias(512, 16, bias_i[0:rows, a, 512:528], 3e38, m).then_inc(na_sb, 1)
                        elif ninth is not None:
                            own.mark(dve.memset(mx0[:, s % 2, :], 3e38))
                            add_bias(0, 592, bias_i[:, a, :], 3e38, m).then_inc(na_sb, 1)
                        else:
                            own.mark(add_bias(512, 16, bias_i[:, a, 512:528], 3e38, mx0[:, s % 2, :]))
                            own.settle(dve)
                            apart(dve)
                            add_bias(0, 512, bias_e[:, a, r0 - 1:r0 + 7, :].rearrange("p t k -> p (t k)"),
                                     mx0[:, s % 2, :], m).then_inc(na_sb, 1)
                    if 0 <= s - 3 < NS:
                        na_mix_part(u, s - 3)
                own.leave(UNITS)

            dper = 2 * DS
            with dve.Fori(0, UNITS) as u:
                own.enter(u, dper + 10)
                dve.wait_ge(qk_evac, 8 * u + 8 * UNITS + 8)
                dve.wait_ge(swp_in, 128 * (u + 1))
                for raw_t, swp, dst in ((q_raw, q_swp, qT), (k_raw, k_swp, kT)):
                    own.mark(dve.tensor_tensor(dst[:, :], raw_t[:, :], cos[:, :], ALU.mult))
                    own.mark(dve.tensor_tensor(swp[:, :], swp[:, :], sin[:, :], ALU.mult))
                    own.settle(dve)
                    dve.tensor_tensor(dst[:, :], dst[:, :], swp[:, :], ALU.add).then_inc(qk_rot, 1)
                evac_v(u * 12 + 12 * UNITS, u * 4 + 4 * UNITS)
                dve.wait_ge(df_ms, u + 1)
                for t0, nt, rows in ((0, FULL, P), (FULL, 1, TAIL)):
                    src = ps[0:rows, 0:2 * BANK].rearrange("p (c n) -> p c n", c=2)
                    own.mark(dve.tensor_scalar(nsm[0:rows, :, t0 * N_META:(t0 + nt) * N_META],
                                               src[:, :, t0 * N_META:(t0 + nt) * N_META], -1.0, None, ALU.mult))
                own.settle(dve)
                dve.sem_inc(df_msn, 1)
                for t0, nt, rows in ((0, FULL, P), (FULL, 1, TAIL)):
                    for c in range(2):
                        own.mark(dve.tensor_reduce(nmm[0:rows, c, t0:t0 + nt],
                                                   nsm[0:rows, c, t0 * N_META:(t0 + nt) * N_META]
                                                   .rearrange("p (t m) -> p t m", m=N_META), AX.X, ALU.min))
                own.settle(dve)
                for s in range(DS + 4):
                    if 0 <= s - 2 < DS:
                        n = s - 2
                        t, rows, keep, k0, kt = DF[n]
                        dve.wait_ge(df_t, u * DS + n + 1)
                        if n >= 2:
                            dve.wait_ge(df_o, u * DS + n - 1)
                        if kt > 4:
                            dve.tensor_copy(et_df[:, n % 2, 4 * P:8 * P].rearrange("p (j r) -> p j r", r=P)[:, :, 0:rows],
                                            ps[:, 5 * BANK:6 * BANK].rearrange("p (j r) -> p j r", r=P)[:, :, 0:rows])
                        dve.tensor_copy(et_df[0:N_META, n % 2, 8 * P:8 * P + rows],
                                        ps[0:N_META, 6 * BANK:6 * BANK + rows]).then_inc(df_et_d, 1)
                    if 0 <= s - 1 < DS:
                        n = s - 1
                        t, rows, keep, k0, kt = DF[n]
                        w = kt * P + N_META
                        b = n % 2
                        dve.wait_ge(df_e, 2 * (u * DS + n) + 2)
                        own.mark(dve.reciprocal(rec[0:rows, n % 4, :], ssum[0:rows, n % 4, :]))
                        own.settle(dve)
                        own.mark(dve.tensor_scalar(sr[0:rows, b, :], rec[0:rows, n % 4, 1:2], ssum[0:rows, n % 4, 0:1],
                                                   neglam[0:rows, :], ALU.mult, ALU.mult))
                        own.settle(dve)
                        dve.scalar_tensor_tensor(out=e_df[0:rows, b, 0, 0:w], in0=e_df[0:rows, b, 1, 0:w],
                                                 scalar=sr[0:rows, b, :], in1=e_df[0:rows, b, 0, 0:w],
                                                 op0=ALU.mult, op1=ALU.add).then_inc(df_c, 1)
                    if s < DS:
                        t, rows, keep, k0, kt = DF[s]
                        w = kt * P + N_META
                        if s >= 2:
                            dve.wait_ge(df_e, 2 * (u * DS + s - 1))
                        dve.tensor_copy(e_df[0:rows, s % 2, :, kt * P:w], nsm[0:rows, :, t * N_META:(t + 1) * N_META])
                        for c in range(2):
                            dve.wait_ge(df_s, 2 * (u * DS + s) + c + 1)
                            dve.tensor_scalar(e_df[0:rows, s % 2, c, 0:kt * P],
                                              ps[0:rows, 2 * c * BANK:2 * c * BANK + kt * P], -1.0,
                                              nmm[0:rows, c, t:t + 1], ALU.mult, ALU.min,
                                              accum_out=nmax[0:rows, s % 2, c:c + 1]).then_inc(df_m, 1)
                    if 0 <= s - 3 < DS:
                        n = s - 3
                        t, rows, keep, k0, kt = DF[n]
                        dve.wait_ge(df_o, u * DS + n + 1)
                        if n == DS - 1:
                            dve.wait_ge(df_sq, u * DS + n + CREDIT)
                        dve.tensor_scalar(mix[0:keep, t, bass.ds(NA_W + u * P, P)],
                                          ps[0:keep, 7 * BANK:7 * BANK + P],
                                          rec[0:keep, n % 4, 0:1], None, ALU.mult).then_inc(df_mix, 1)
                own.leave(UNITS)

            dve.wait_ge(df_sq, DS * UNITS + CREDIT)
            keep2 = (1.0 - LAMBDA_INIT) ** 2
            dve.tensor_scalar(ms_d[:, :, :], ms_d[:, :, :], 1.0 / (P * keep2), SUB_EPS / keep2, ALU.mult, ALU.add).then_inc(sub_ms, 1)
            own.mark(dve.memset(aff[:, :], -1.0))
            own.settle(dve)
            dve.wait_ge(sub_rstd, 1)
            own.flat()

            def c_pair(i, bs, rows):
                for b in bs:
                    dve.wait_ge(mT_ready, 2 * i + CREDIT)
                    t = bass.ds(2 * i + b, 1)
                    dve.tensor_tensor(mixs[0:rows, b, NA_W:D].rearrange("p (h f) -> p h f", f=P),
                                      mix[0:rows, t, NA_W:D].rearrange("p o (h f) -> p (o h) f", f=P),
                                      rstd_d[0:rows, t, :].rearrange("p o (h f) -> p (o h) f", f=1)
                                      .to_broadcast([rows, UNITS, P]),
                                      ALU.mult).then_inc(mixs_d, 1)
                for b in bs:
                    dve.wait_ge(mT_ready, 2 * i + b + 1 + CREDIT)
                    src = ps[:, 2 * b * BANK:(2 * b + 2) * BANK].rearrange("p (k r) -> p k r", r=P)
                    dve.tensor_tensor(mixT[:, b, :, 0:rows], src[:, :, 0:rows],
                                      bcast(vec, 2 * KD, [[1, KD], [0, rows]]), ALU.mult).then_inc(mT_evac, 1)
                for b in bs:
                    dve.wait_ge(o_ready, 2 * i + b + 1)
                    dve.wait_ge(xr_in[b], 16 * i + 16)
                    dve.wait_ge(x2_out[b], 16 * i + CREDIT)
                    dve.wait_ge(xn2_ready, 2 * i + CREDIT)
                    off = (4 + 2 * b) * BANK
                    dve.tensor_tensor(x2[0:rows, b, :], ps[0:rows, off:off + D], xr[0:rows, b, :],
                                      ALU.add).then_inc(x2_ready, 1)
                    dve.wait_ge(ss2_ready, 2 * i + b + 1)
                    dve.tensor_scalar(ms2[0:rows, b, :], ms2[0:rows, b, :], 1.0 / D, RMS_EPS,
                                      ALU.mult, ALU.add).then_inc(ms2_ready, 1)
                for b in bs:
                    dve.wait_ge(h2_ready, 2 * i + b + 1 + CREDIT)
                    dve.wait_ge(lg_ready, 2 * i + CREDIT)
                    src = ps[:, 2 * b * BANK:(2 * b + 2) * BANK].rearrange("p (k r) -> p k r", r=P)
                    dve.tensor_tensor(h2T[:, b, :, 0:rows], src[:, :, 0:rows],
                                      bcast(vec, KD, [[1, KD], [0, rows]]), ALU.mult).then_inc(h2_evac, 1)
                for b in bs:
                    dve.wait_ge(lg_ready, 2 * i + b + 1 + CREDIT)
                    off = (4 + 2 * b) * BANK
                    dve.tensor_reduce(nmax[0:rows, b, 0:1], ps[0:rows, off:off + N_EXP], AX.X, ALU.max,
                                      negate=True).then_inc(lg_max, 1)
                    dve.wait_ge(lg_exp, 2 * i + b + 1)
                    own.mark(dve.reciprocal(rec[0:rows, b, 0:1], ssum[0:rows, b, 0:1]))
                    own.settle(dve)
                    dve.tensor_scalar(lg_a[0:rows, b, :], lg_e[0:rows, b, :], rec[0:rows, b, 0:1], None,
                                      ALU.mult).then_inc(lg_aff, 1)

            with dve.Fori(0, PAIRS) as i:
                own.enter(i, 2)
                c_pair(i, (0, 1), P)
                own.leave(PAIRS)
            c_pair(PAIRS, (0,), TAIL)
            own.flat()

            dve.wait_ge(affT_evac, NT + CREDIT)
            own.mark(dve.tensor_copy(aff[0:N_EXP, N_META:N_META + N_PROMPT], aff_all[:, 0:N_PROMPT]))
            own.mark(dve.tensor_copy(aff[32:48, N_META:N_META + N_SAMPLE], aff_all[:, N_PROMPT:N_REAL]))
            own.mark(dve.tensor_copy(aff[0:N_EXP, 0:N_META], aff_all[:, N_REAL:N_REAL + N_META]))
            own.mark(dve.tensor_copy(aff[32:48, 0:N_META], aff_all[:, N_REAL + N_META:NTOK]))
            own.settle(dve)
            for r in range(-(-CAP_P // 8)):
                top = top_v[:, 8 * r:8 * r + 8]
                own.mark(dve.max(top, aff[:, :]))
                own.settle(dve)
                own.mark(dve.max_index(top_i[:, 8 * r:8 * r + 8], top, aff[:, :]))
                own.mark(dve.match_replace(aff[:, :], top, aff[:, :], -1.0))
                own.settle(dve)
            own.mark(dve.tensor_copy(top_f[:, :], top_i[:, :]))
            own.settle(dve)
            for p0, first, meta0, cap, s0 in ((0, 0, N_REAL, CAP_P, 0), (32, N_PROMPT, N_REAL + N_META, CAP_S, CAP_P)):
                lanes = slice(p0, p0 + N_EXP)
                shift = first - N_META
                own.mark(dve.tensor_scalar(top_m[lanes, 0:cap], top_f[lanes, 0:cap], float(N_META),
                                           float(meta0 - shift), ALU.is_lt, ALU.mult))
                own.settle(dve)
                own.mark(dve.scalar_tensor_tensor(out=slot_r[:, s0:s0 + cap], in0=top_f[lanes, 0:cap],
                                                  scalar=float(shift), in1=top_m[lanes, 0:cap],
                                                  op0=ALU.add, op1=ALU.add))
                own.mark(dve.tensor_copy(slot_g[:, s0:s0 + cap], top_v[lanes, 0:cap]))
            own.settle(dve)
            dve.memset(mx0[:, 0, :], 0.0).then_inc(slots_ready, 1)
            dve.wait_ge(slotT_ready, 1)
            for hh in range(2):
                own.mark(dve.tensor_copy(idxT[:, hh, 0:N_EXP], ps[0:HS, hh * P:hh * P + N_EXP]))
                own.mark(dve.tensor_copy(gateT[:, hh, 0:N_EXP], ps[0:HS, (2 + hh) * P:(2 + hh) * P + N_EXP]))
            own.settle(dve)
            dve.memset(mx0[:, 0, :], 0.0).then_inc(idx_ready, 1)
            own.flat()

            def split_lo(e, n):
                e, n = (e + 1, n - PIECES) if n >= PIECES else (e, n)
                dve.wait_ge(hi_done, PIECES * e + n + 1)
                dve.tensor_tensor(w_lo[:, n % NW, :], raw[:, n % NRAW, :], w_hi[:, n % NW, :].bitcast(f32),
                                  ALU.subtract).then_inc(lo_done, 1)

            def hidden_lo(e, m):
                dve.wait_ge(hid_hi, NF * e + m + 1)
                dve.tensor_tensor(hid[:, m, 1, :], hf[:, m % 2, :], hid[:, m, 0, :].bitcast(f32),
                                  ALU.subtract).then_inc(hid_lo, 1)

            def xe_lo_part(turn):
                for k in range(KD):
                    dve.wait_ge(xe_hi_done, turn * KD + 2 * (k // 2) + 2)
                    off = (k // 2) * BANK + (k % 2) * SLOTS
                    dve.scalar_tensor_tensor(out=xe[:, k, 1, :], in0=ps[:, off:off + SLOTS],
                                             scalar=vec[:, KD + k:KD + k + 1], in1=xe[:, k, 0, :].bitcast(f32),
                                             op0=ALU.mult, op1=ALU.subtract).then_inc(xe_lo_done, 1)

            def result_rows(e, half):
                dve.wait_ge(yt_ready, 2 * e + half + 1)
                dve.wait_ge(added, e + 1)
                dve.wait_ge(gate_cp, e + 1)
                dve.tensor_scalar(ye[:, 1, half * 512:(half + 1) * 512], ps[0:HS, 7 * BANK:8 * BANK],
                                  gate_cur[:, 1:2], None, ALU.mult).then_inc(ye_d, 1)

            def expert(e, last):
                dve.wait_ge(ye_a, 2 * e + 1)
                dve.wait_ge(ye_d, 2 * e + 1)
                dve.tensor_copy(gate_cur[:, :].rearrange("p (h o) -> p h o", o=1),
                                gateT[:, :, bass.ds(e, 1)]).then_inc(gate_cp, 1)
                for m in range(NF):
                    i = NF * e + m
                    dve.wait_ge(part_done, i + 1)
                    src = ps[:, 2 * (m % 2) * BANK:2 * (m % 2 + 1) * BANK].rearrange("p (j n) -> p j n", j=2)
                    dve.tensor_tensor(gusum[:, m % 2, :, :], src[:, :, 0:SLOTS], part[:, m % 2, :, :],
                                      ALU.add).then_inc(sum_done, 1)
                    if m > 0:
                        hidden_lo(e, m - 1)
                    if m < NF - 1:
                        split_lo(e, m + LEAD - 1)
                    dve.wait_ge(silu_done, i + 1)
                    dve.tensor_tensor(hf[:, m % 2, :], sil[:, m % 2, :], gusum[:, m % 2, 1, :],
                                      ALU.mult).then_inc(hf_done, 1)
                hidden_lo(e, NF - 1)
                split_lo(e, NF - 1 + LEAD - 1)
                for d in range(KD):
                    i = KD * e + d
                    if not last or d < KD - LEAD + 1:
                        split_lo(e, GU + d + LEAD - 1)
                    if d == 4 and not last:
                        xe_lo_part(e + 1)
                    if d == 5:
                        result_rows(e, 0)
                    dve.wait_ge(ypart_done, i + 1)
                    off = (4 + d % 2) * BANK
                    dve.tensor_tensor(yT[:, d, :], ps[:, off:off + SLOTS], y_part[:, d % 2, :],
                                      ALU.add).then_inc(yT_done, 1)
                result_rows(e, 1)

            dve.sem_inc(lo_done, NRAW)
            dve.sem_inc(sum_done, 1)
            dve.sem_inc(yT_done, 1)
            dve.sem_inc(ye_d, 1)
            for n in range(LEAD - 1):
                split_lo(0, n)
            xe_lo_part(0)
            with dve.Fori(0, N_EXP - 1) as e:
                expert(e, False)
            expert(N_EXP - 1, True)

            dve.wait_ge(g_in, 16)
            with dve.Fori(0, PAIRS) as i:
                for b in range(2):
                    dve.wait_ge(ss3, 2 * i + b + 1)
                    dve.tensor_scalar(ms2[:, b, :], ms2[:, b, :], 1.0 / D, RMS_EPS, ALU.mult, ALU.add).then_inc(ms3, 1)
                for b in range(2):
                    dve.wait_ge(rstd3, 2 * i + b + 1 + CREDIT)
                    dve.wait_ge(y_out[b], 16 * i + CREDIT)
                    dve.scalar_tensor_tensor(out=yo[:, b, :], in0=xf[:, bass.ds(2 * i + b, 1), :].rearrange("p o d -> p (o d)"),
                                             scalar=rstd[:, b, :], in1=g_fin[:, :], op0=ALU.mult,
                                             op1=ALU.mult).then_inc(y3, 1)

        @block.tensor
        def _(pe):
            for started in (xT_ready, pj_ready, mT_ready, h2_ready, lg_ready, affT_ready):
                pe.sem_inc(started, CREDIT)
            pe.wait_ge(const_in, 16 * 5)

            def a_tiles(i, bs, rows):
                for b in bs:
                    pe.wait_ge(xn_ready, 2 * i + b + 1 + CREDIT)
                    pe.wait_ge(h_ready, 2 * i + CREDIT)
                    for k in range(KD):
                        off = 2 * b * BANK + k * P
                        ins = pe.transpose(ps[:, off:off + rows], xn[0:rows, b, k * P:(k + 1) * P], ident[0:rows, 0:rows])
                    ins.then_inc(xT_ready, 1)

            with pe.Fori(0, PAIRS) as i:
                a_tiles(i, (0, 1), P)
            a_tiles(PAIRS, (0,), TAIL)

            def project(u, uu):
                pe.wait_ge(w_qkv_in, 48 * (uu + 1))
                pe.wait_ge(v_evac, 4 * uu + CREDIT)
                for n in range(8):
                    c, which = n // 2, n % 2
                    if n >= 2:
                        pe.wait_ge(qk_evac, 8 * uu + n - 1)
                    off = (6 + n % 2) * BANK
                    for k in range(KD):
                        ins = pe.matmul(ps[:, off:off + QCH], wqkv[:, k, which * P:(which + 1) * P],
                                        hT[:, k, c * QCH:(c + 1) * QCH], start=(k == 0), stop=(k == KD - 1))
                    ins.then_inc(pj_ready, 1)
                for g in range(4):
                    if g < 2:
                        pe.wait_ge(qk_evac, 8 * uu + 7 + g)
                    else:
                        pe.wait_ge(v_evac, 4 * uu + g - 1 + CREDIT)
                    for t in range(4 * g, min(4 * g + 4, NT)):
                        rows = P if t < FULL else TAIL
                        off = (6 + g % 2) * BANK + (t - 4 * g) * P
                        for k in range(KD):
                            ins = pe.matmul(ps[0:rows, off:off + P], hT[:, k, t * P:t * P + rows],
                                            wqkv[:, k, 2 * P:3 * P], start=(k == 0), stop=(k == KD - 1))
                    ins.then_inc(pj_ready, 1)

            et_a_count = [sum(1 for x in NA[:n + 1] if x[3] is not None) for n in range(NS)]
            per_a = et_a_count[-1]
            pe.wait_ge(h_ready, NT + CREDIT)
            with pe.Fori(0, UNITS) as u:
                pe.wait_ge(na_mix, NS * u + CREDIT)
                project(u, u)
                pe.wait_ge(qk_evac, 8 * (u + 1))
                pe.wait_ge(v_evac, 4 * (u + 1) + CREDIT)
                for s in range(NS + 2):
                    if s < NS:
                        a, t, rows, k0, ninth, _ = NA[s]
                        if s >= 2:
                            pe.wait_ge(na_sb, u * NS + s - 1 + CREDIT)
                        if rows < P:
                            apart(pe)
                        f = slice(a * DH, a * DH + DH)
                        q = qT[f, t * P:t * P + rows]
                        c0 = (s % 2) * 2 * BANK
                        if k0 is not None:
                            pe.matmul(ps[0:rows, c0:c0 + 512], q, kT[f, k0 * P:(k0 + 4) * P], start=True, stop=True)
                        ins = pe.matmul(ps[0:rows, c0 + 512:c0 + 528], q, kT[f, N_REAL:N_REAL + N_META],
                                        start=True, stop=True)
                        if ninth is not None:
                            ins = pe.matmul(ps[0:rows, c0 + 528:c0 + 592], q, kT[f, ninth * P:ninth * P + 64],
                                            start=True, stop=True)
                        ins.then_inc(na_s, 1)
                    if 0 <= s - 1 < NS:
                        n = s - 1
                        a, t, rows, k0, ninth, _ = NA[n]
                        b = n % 2
                        pe.wait_ge(na_e, u * NS + n + 1)
                        if n >= 1:
                            pe.wait_ge(na_et_a, u * per_a + et_a_count[n - 1])
                            pe.wait_ge(na_et_d, u * NS + n)
                        if rows < P:
                            apart(pe)
                        if k0 is not None:
                            for j in range(4):
                                pe.transpose(ps[:, 4 * BANK + j * P:4 * BANK + (j + 1) * P],
                                             e_na[:, b, j * P:(j + 1) * P], ident[:, :])
                        ins = pe.transpose(ps[0:N_META, 5 * BANK:5 * BANK + rows], e_na[0:rows, b, 512:528],
                                           ident[0:rows, 0:rows])
                        if ninth is not None:
                            ins = pe.transpose(ps[0:64, 5 * BANK + P:5 * BANK + 2 * P], e_na[:, b, 528:592], ident[:, :])
                        ins.then_inc(na_t, 1)
                    if 0 <= s - 2 < NS:
                        n = s - 2
                        a, t, rows, k0, ninth, _ = NA[n]
                        b = n % 2
                        pe.wait_ge(na_et_a, u * per_a + et_a_count[n])
                        pe.wait_ge(na_et_d, u * NS + n + 1)
                        if n >= 2:
                            pe.wait_ge(na_mix, u * NS + n - 1 + CREDIT)
                        if rows < P:
                            apart(pe)
                        o = ps[0:rows, (6 + b) * BANK:(6 + b) * BANK + DH]
                        f = slice(a * DH, a * DH + DH)
                        pairs = [(et_na[0:N_META, b, 512:512 + rows], v[0:N_META, FULL, f])]
                        if k0 is not None:
                            pairs += [(et_na[:, b, j * P:(j + 1) * P], v[:, k0 + j, f]) for j in range(4)]
                        if ninth is not None:
                            pairs += [(et_na[0:64, b, 640:768], v[0:64, ninth, f])]
                        for j, (pt, vv) in enumerate(pairs):
                            ins = pe.matmul(o, pt, vv, start=(j == 0), stop=(j == len(pairs) - 1))
                        ins.then_inc(na_o, 1)

            pe.wait_ge(na_mix, NS * UNITS + CREDIT)
            with pe.Fori(0, UNITS) as u:
                pe.wait_ge(df_et_d, DS * u + CREDIT)
                pe.wait_ge(df_mix, DS * u + CREDIT)
                project(u, u + UNITS)
                pe.wait_ge(qk_rot, 2 * (u + 1))
                pe.wait_ge(v_evac, 4 * (u + 1) + 4 * UNITS + CREDIT)
                for c in range(2):
                    for t in range(NT):
                        rows = P if t < FULL else TAIL
                        f = slice(c * DH, c * DH + DH)
                        o = c * BANK + t * N_META
                        ins = pe.matmul(ps[0:rows, o:o + N_META], qT[f, t * P:t * P + rows],
                                        kT[f, N_REAL:N_REAL + N_META], start=True, stop=True)
                ins.then_inc(df_ms, 1)
                pe.wait_ge(df_msn, u + 1)
                for s in range(DS + 2):
                    if s < DS:
                        t, rows, keep, k0, kt = DF[s]
                        for c in range(2):
                            if s >= 1:
                                pe.wait_ge(df_m, 2 * (u * DS + s - 1) + c + 1)
                            if rows < P:
                                apart(pe)
                            f = slice(c * DH, c * DH + DH)
                            q = qT[f, t * P:t * P + rows]
                            o = 2 * c * BANK
                            for j in range(kt // 4):
                                ins = pe.matmul(ps[0:rows, o + j * 512:o + (j + 1) * 512], q,
                                                kT[f, (k0 + 4 * j) * P:(k0 + 4 * j + 4) * P], start=True, stop=True)
                            ins.then_inc(df_s, 1)
                    if 0 <= s - 1 < DS:
                        n = s - 1
                        t, rows, keep, k0, kt = DF[n]
                        b = n % 2
                        pe.wait_ge(df_c, u * DS + n + 1)
                        if n >= 1:
                            pe.wait_ge(df_et_a, u * DS + n)
                            pe.wait_ge(df_et_d, u * DS + n + CREDIT)
                        if rows < P:
                            apart(pe)
                        for j in range(kt):
                            pe.transpose(ps[:, 4 * BANK + j * P:4 * BANK + j * P + rows],
                                         e_df[0:rows, b, 0, j * P:(j + 1) * P], ident[0:rows, 0:rows])
                        pe.transpose(ps[0:N_META, 6 * BANK:6 * BANK + rows],
                                     e_df[0:rows, b, 0, kt * P:kt * P + N_META], ident[0:rows, 0:rows]).then_inc(df_t, 1)
                    if 0 <= s - 2 < DS:
                        n = s - 2
                        t, rows, keep, k0, kt = DF[n]
                        b = n % 2
                        pe.wait_ge(df_et_a, u * DS + n + 1)
                        pe.wait_ge(df_et_d, u * DS + n + 1 + CREDIT)
                        if n >= 1:
                            pe.wait_ge(df_mix, u * DS + n + CREDIT)
                        if rows < P:
                            apart(pe)
                        o = ps[0:rows, 7 * BANK:7 * BANK + P]
                        pe.matmul(o, et_df[0:N_META, b, 8 * P:8 * P + rows], v[0:N_META, FULL, :], start=True, stop=False)
                        for j in range(kt):
                            ins = pe.matmul(o, et_df[:, b, j * P:j * P + rows], v[:, k0 + j, :], start=False,
                                            stop=(j == kt - 1))
                        ins.then_inc(df_o, 1)

            pe.wait_ge(w_out_in, 32)
            pe.wait_ge(df_mix, DS * UNITS + CREDIT)

            def c_pair(i, bs, rows):
                for b in bs:
                    pe.wait_ge(mixs_a, 2 * i + b + 1)
                    pe.wait_ge(mixs_d, 2 * i + b + 1)
                    pe.wait_ge(h2_evac, 2 * i + CREDIT)
                    for k in range(KD):
                        off = 2 * b * BANK + k * P
                        ins = pe.transpose(ps[:, off:off + rows], mixs[0:rows, b, k * P:(k + 1) * P], ident[0:rows, 0:rows])
                    ins.then_inc(mT_ready, 1)
                for b in bs:
                    pe.wait_ge(mT_evac, 2 * i + b + 1)
                    pe.wait_ge(affT_evac, 2 * i + CREDIT)
                    for n in range(2):
                        off = (4 + 2 * b + n) * BANK
                        for k in range(KD):
                            ins = pe.matmul(ps[0:rows, off:off + 512], mixT[:, b, k, 0:rows],
                                            w_out_sb[:, k, n * 512:(n + 1) * 512], start=(k == 0), stop=(k == KD - 1))
                    ins.then_inc(o_ready, 1)
                for b in bs:
                    pe.wait_ge(xn2_ready, 2 * i + b + 1 + CREDIT)
                    for k in range(KD):
                        off = 2 * b * BANK + k * P
                        ins = pe.transpose(ps[:, off:off + rows], xn2[0:rows, b, k * P:(k + 1) * P], ident[0:rows, 0:rows])
                    ins.then_inc(h2_ready, 1)
                for b in bs:
                    pe.wait_ge(h2_evac, 2 * i + b + 1 + CREDIT)
                    off = (4 + 2 * b) * BANK
                    for k in range(KD):
                        ins = pe.matmul(ps[0:rows, off:off + N_EXP], h2T[:, b, k, 0:rows], w_rt[:, k, :],
                                        start=(k == 0), stop=(k == KD - 1))
                    ins.then_inc(lg_ready, 1)
                for b in bs:
                    pe.wait_ge(lg_aff, 2 * i + b + 1)
                    off = (4 + 2 * b) * BANK + 128
                    pe.transpose(ps[0:N_EXP, off:off + rows], lg_a[0:rows, b, :], ident[0:rows, 0:rows]).then_inc(affT_ready, 1)

            with pe.Fori(0, PAIRS) as i:
                c_pair(i, (0, 1), P)
            c_pair(PAIRS, (0,), TAIL)

            pe.wait_ge(slots_ready, 1)
            for n, src in enumerate((slot_r, slot_g)):
                for hh in range(2):
                    off = (2 * n + hh) * P
                    ins = pe.transpose(ps[0:HS, off:off + N_EXP], src[:, hh * HS:(hh + 1) * HS], ident[0:N_EXP, 0:N_EXP])
            ins.then_inc(slotT_ready, 1)

            def gathered_to_columns(turn):
                pe.wait_ge(gather_in, 32 * (turn + 1))
                for k in range(KD):
                    for hh in range(2):
                        off = (k // 2) * BANK + (k % 2) * SLOTS + hh * HS
                        ins = pe.transpose(ps[:, off:off + HS], xg[:, hh, k * P:(k + 1) * P], ident[0:HS, 0:HS])
                    if k % 2:
                        ins.then_inc(xgT_ready, 1)

            def three(out, cols, slot, x, first, last):
                pe.matmul(out, w_hi[:, slot, cols], x.rearrange("p h n -> p (h n)"), start=first, stop=False)
                return pe.matmul(out[:, 0:SLOTS], w_lo[:, slot, cols], x[:, 0, :], start=False, stop=last)

            def expert(e, last):
                pe.wait_ge(xe_lo_done, KD * (e + 1))
                for m in range(NF):
                    i = NF * e + m
                    pe.wait_ge(sum_done, i + CREDIT)
                    for j in range(2):
                        n = 2 * (m // 2) + j
                        if m % 2 == 0:
                            pe.wait_ge(lo_done, PIECES * e + n + 1 + NRAW)
                        bank = 2 * (m % 2) + j
                        for k in range(KD):
                            c0 = k * FCH + (m % 2) * P
                            ins = three(ps[:, bank * BANK:bank * BANK + 2 * SLOTS], slice(c0, c0 + P), n % NW,
                                        xe[:, k, :, :], k == 0, k == KD - 1)
                    ins.then_inc(gu_ready, 1)
                for d in range(KD):
                    i = KD * e + d
                    n = GU + d
                    pe.wait_ge(yT_done, i + CREDIT)
                    pe.wait_ge(lo_done, PIECES * e + n + 1 + NRAW)
                    bank = 4 + d % 2
                    for m in range(NF):
                        if d == 0 and m >= NF - 5:
                            pe.wait_ge(hid_lo, NF * e + m + 1)
                        ins = three(ps[:, bank * BANK:bank * BANK + 2 * SLOTS], slice(m * P, (m + 1) * P), n % NW,
                                    hid[:, m, :, :], m == 0, m == NF - 1)
                    ins.then_inc(dn_ready, 1)
                    if d == 3 and not last:
                        pe.wait_ge(sum_done, NF * (e + 1) + 1 + CREDIT)
                        gathered_to_columns(e + 1)
                    if d > 0:
                        result_columns(e, d - 1)
                result_columns(e, KD - 1)

            def result_columns(e, d):
                pe.wait_ge(yT_done, KD * e + d + 2 + CREDIT)
                if d % 4 == 0:
                    pe.wait_ge(ye_a, 2 * e + d // 4 + 1)
                    pe.wait_ge(ye_d, 2 * e + d // 4 + 1)
                for hh in range(2):
                    off = (6 + hh) * BANK + (d % 4) * P
                    ins = pe.transpose(ps[0:HS, off:off + P], yT[:, d, hh * HS:(hh + 1) * HS], ident[:, :])
                if d % 4 == 3:
                    ins.then_inc(yt_ready, 1)

            pe.sem_inc(dn_ready, KD)
            gathered_to_columns(0)
            with pe.Fori(0, N_EXP - 1) as e:
                expert(e, False)
            expert(N_EXP - 1, True)

        @block.gpsimd
        def _(pool):
            def rsqrt(out, in_, expo):
                return pool.tensor_tensor(out, in_, expo, ALU.pow)

            for started in (rstd_ready, rstd2_ready, rstd3):
                pool.sem_inc(started, CREDIT)
            pool.wait_ge(consts_dve, 1)

            def stats(i, bs, rows, ready, src, done):
                for b in bs:
                    pool.wait_ge(ready, 2 * i + b + 1)
                    rsqrt(rstd[0:rows, b, :], src[0:rows, b, :], half_neg[0:rows, 0:1]).then_inc(done, 1)

            with pool.Fori(0, PAIRS) as i:
                stats(i, (0, 1), P, ms_ready, ms, rstd_ready)
            stats(PAIRS, (0,), TAIL, ms_ready, ms, rstd_ready)

            pool.wait_ge(sub_ms, 1)
            rsqrt(rstd_d[:, :, :].rearrange("p t u -> p (t u)"), ms_d[:, :, :].rearrange("p t u -> p (t u)"),
                  bcast(half_neg, 0, [[0, NT * UNITS]])).then_inc(sub_rstd, 1)

            with pool.Fori(0, PAIRS) as i:
                stats(i, (0, 1), P, ms2_ready, ms2, rstd2_ready)
            stats(PAIRS, (0,), TAIL, ms2_ready, ms2, rstd2_ready)

            pool.wait_ge(idx_ready, 1)
            for b in range(2):
                full = 16 * (PAIRS + (1 - b))
                pool.wait_ge(xn2_out[b], full + CREDIT)
                pool.wait_ge(x2_out[b], full + CREDIT)

            def gather(turn):
                pool.tensor_copy(idx_gather[:, :].rearrange("p (h o) -> p h o", o=1),
                                 idxT[:, :, bass.ds(turn, 1)]).then_inc(idx_cp, 1)
                pool.wait_ge(idx_cp, turn + 1)
                apart(pool)
                for hh in range(2):
                    pool.indirect_dma_start(
                        out=xg[:, hh, :], out_offset=None, in_=h_d,
                        in_offset=bass.IndirectOffsetOnAxis(ap=idx_gather[:, hh:hh + 1], axis=0)).then_inc(gather_in, 16)

            def scatter(e):
                pool.tensor_copy(idx_scatter[:, :].rearrange("p (h o) -> p h o", o=1),
                                 idxT[:, :, bass.ds(e, 1)]).then_inc(idx_sc, 1)
                pool.wait_ge(idx_sc, e + 1)
                for hh, done in ((0, ye_a), (1, ye_d)):
                    pool.wait_ge(done, 2 * (e + 1) + 1)
                    apart(pool)
                    pool.indirect_dma_start(
                        out=acc_d, out_offset=bass.IndirectOffsetOnAxis(ap=idx_scatter[:, hh:hh + 1], axis=0),
                        in_=ye[:, hh, :], in_offset=None, compute_op=ALU.add).then_inc(scatter_out, 16)
                pool.wait_ge(scatter_out, 32 * (e + 1))
                pool.sem_inc(added, 1)

            pool.sem_inc(added, 1)
            gather(0)
            with pool.Fori(0, N_EXP - 1) as e:
                pool.wait_ge(xgT_ready, (KD // 2) * (e + 1))
                gather(e + 1)
                scatter(e)
            scatter(N_EXP - 1)

            with pool.Fori(0, PAIRS) as i:
                stats(i, (0, 1), P, ms3, ms2, rstd3)


_OUT = "y_dram"


def kernel(**inputs):
    import concourse.bacc as bacc
    from concourse.bass_utils import run_bass_kernel_spmd

    a = {n: np.ascontiguousarray(x) for n, x in inputs.items()}
    nc = bacc.Bacc("TRN2", target_bir_lowering=False, num_devices=1)
    meta_pos = np.arange(N_META)
    pos = np.concatenate([N_META + np.arange(N_PROMPT), N_META + np.arange(N_SAMPLE), meta_pos, meta_pos])
    inv = np.float32(1.0) / (np.float32(10000.0) ** (np.arange(0, DH, 2, dtype=np.float32) / np.float32(DH)))
    ang = inv[:, None] * pos.astype(np.float32)[None, :]
    c, s = np.cos(ang), np.sin(ang)
    rope = np.stack([np.concatenate([c, c, c, c]), np.concatenate([-s, s, -s, s])]).astype(np.float32)
    ones = np.ones((P, KD // 2), np.float32)
    arrays = {
        "x_all": np.concatenate([a["x_prompt"][0], a["x_sample"][0], a["meta_tokens"], a["meta_tokens"]]),
        "w_in": a["w_in"][0],
        "w_out": a["w_out"][0],
        "w_router": a["w_router"][0].reshape(KD, P, N_EXP).transpose(1, 0, 2),
        "w_gate": a["w_gate"][0],
        "w_up": a["w_up"][0],
        "w_down": a["w_down"][0],
        "rpb": a["na_rpb"][0],
        "meta_bias": a["na_meta_bias"][0],
        "lambdas": np.stack([a[f"lambda_{n}"][0] for n in ("q1", "k1", "q2", "k2")]),
        "vecs": np.concatenate([a["norm_mix"][0].reshape(KD, P).T, a["norm_ffn"][0].reshape(KD, P).T, ones,
                                np.repeat(a["diff_subln"][0][:, None], KD // 2, axis=1)], axis=1),
        "final_norm": a["final_norm"],
        "rope": rope,
        "ident": np.eye(P, dtype=np.float32),
    }
    arrays = {f"{n}_dram": np.ascontiguousarray(x) for n, x in arrays.items()}
    aps = [nc.dram_tensor(n, x.shape, mybir.dt.from_np(x.dtype), kind="ExternalInput").ap() for n, x in arrays.items()]
    out = nc.dram_tensor(_OUT, (N_REAL, D), f32, kind="ExternalOutput").ap()
    build(nc, *aps, out)
    r = run_bass_kernel_spmd(nc, [arrays], core_ids=[0])
    got = r.results[0][_OUT]
    return got[None, :N_PROMPT], got[None, N_PROMPT:]
```
